# Optimizing a Trainium2 kernel written in Bass

```python
import jax, jax.numpy as jnp
from jax import lax
import numpy as np

D_MODEL = 1024
BATCH = 1
SEQ = 128
DEPTH = 2
DEC_BATCH = 1
DEC_SEQ = 512
PAST_LEN = 128

GRID_W = 64
RMS_EPS = 1e-6
LN_EPS = 1e-5
N_MOD = 6
N_BRANCH = 3

RW_HEADS = 8
RW_HEAD_DIM = 64
RW_WIDTH = RW_HEADS * RW_HEAD_DIM
RW_LORA_W = 64
RW_LORA_A = 64
RW_LORA_G = 128
RW_GN_EPS = 64e-5
RW_SIZES = (RW_WIDTH, RW_WIDTH, RW_WIDTH, RW_LORA_W, RW_LORA_W, RW_LORA_A, RW_LORA_A, RW_LORA_G)
RW_COLS = sum(RW_SIZES)

CONV_WIDTH = 512
CONV_KERNEL = 31

ATT_HEADS = 8
ATT_KV_HEADS = 2
ATT_GROUP = ATT_HEADS // ATT_KV_HEADS
HEAD_DIM = 64
ROT_HALF = HEAD_DIM // 2
ROPE_THETA = 10000.0
Q_BLOCK = 128

PEER_HEADS = 8
PEER_N_KEYS = 128
PEER_N_EXPERTS = PEER_N_KEYS * PEER_N_KEYS
PEER_KEY_DIM = 128
PEER_HALF = PEER_KEY_DIM // 2
PEER_TOPK = 16
PEER_CHUNK = 128

IN_SIZES = (RW_COLS, 2 * CONV_WIDTH, ATT_HEADS * HEAD_DIM, ATT_KV_HEADS * HEAD_DIM, ATT_KV_HEADS * HEAD_DIM, N_BRANCH * D_MODEL)
IN_COLS = sum(IN_SIZES)

kernel_name = 'hybrid_rwkv7_conformer_gqa_peer_dit_step'

def _split(z, sizes):
    parts, start = [], 0
    for s in sizes:
        parts.append(z[..., start:start + s])
        start += s
    return parts

def rms_norm(x):
    xf = x.astype(jnp.float32)
    return (xf * lax.rsqrt(jnp.mean(xf * xf, axis=-1, keepdims=True) + RMS_EPS)).astype(x.dtype)

def head_rms_norm(x, g):
    xf = x.astype(jnp.float32)
    return (xf * lax.rsqrt(jnp.mean(xf * xf, axis=-1, keepdims=True) + RMS_EPS) * g).astype(x.dtype)

def layer_norm(x, w, b):
    xf = x.astype(jnp.float32)
    mu = jnp.mean(xf, axis=-1, keepdims=True)
    var = jnp.mean(jnp.square(xf - mu), axis=-1, keepdims=True)
    return ((xf - mu) * lax.rsqrt(var + LN_EPS) * w + b).astype(x.dtype)

def modulation(cond, w, b):
    return jnp.split(jax.nn.silu(cond) @ w + b, N_MOD, axis=-1)

def modulate(x, shift, scale):
    return rms_norm(x) * (1 + scale) + shift

def token_shift3(z, mu_prev, mu_next):
    z_prev = jnp.pad(z[:, :-1], ((0, 0), (1, 0), (0, 0)))
    z_next = jnp.pad(z[:, 1:], ((0, 0), (0, 1), (0, 0)))
    return z + mu_prev * (z_prev - z) + mu_next * (z_next - z)

def wkv_scan(r, w, k, v, kk, a, s0, reverse):
    def step(s, inp):
        r_t, w_t, k_t, v_t, kk_t, a_t = inp
        s_kk = jnp.einsum('bhvk,bhk->bhv', s, kk_t)
        s = (s * w_t[:, :, None, :]
             - s_kk[..., None] * (kk_t * a_t)[:, :, None, :]
             + v_t[..., None] * k_t[:, :, None, :])
        return s, jnp.einsum('bhvk,bhk->bhv', s, r_t)
    xs = tuple(jnp.moveaxis(t, 1, 0) for t in (r, w, k, v, kk, a))
    s_fin, out = lax.scan(step, s0, xs, reverse=reverse)
    return jnp.moveaxis(out, 0, 1), s_fin

def rwkv_mixer(z, lp, s0):
    B, T, _ = z.shape
    z = token_shift3(z, lp['shift_mu_prev'], lp['shift_mu_next'])
    r, k, v, zw_f, zw_b, za_f, za_b, zg = _split(z, RW_SIZES)
    heads = lambda t: t.astype(jnp.float32).reshape(B, T, RW_HEADS, RW_HEAD_DIM)
    kk = heads(k * lp['rw_k_k'])
    kk = kk * lax.rsqrt(jnp.sum(kk * kk, axis=-1, keepdims=True) + 1e-12)
    outs, finals = [], []
    for d, (zw, za) in enumerate(((zw_f, za_f), (zw_b, za_b))):
        w_raw = (lp['rw_w0'][d] + jnp.tanh(zw) @ lp['rw_w2'][d]).astype(jnp.float32)
        decay = jnp.exp(-jnp.exp(-jax.nn.softplus(-w_raw) - 0.5))
        a = jax.nn.sigmoid(lp['rw_a0'][d] + za @ lp['rw_a2'][d])
        k_d = k * (1 + (a - 1) * lp['rw_k_a'])
        o, s_fin = wkv_scan(heads(r), heads(decay), heads(k_d), heads(v), kk, heads(a),
                            s0[:, d].astype(jnp.float32), reverse=(d == 1))
        outs.append(o)
        finals.append(s_fin)
    o = outs[0] + outs[1]
    mu = jnp.mean(o, axis=-1, keepdims=True)
    var = jnp.mean(jnp.square(o - mu), axis=-1, keepdims=True)
    o = ((o - mu) * lax.rsqrt(var + RW_GN_EPS)).reshape(B, T, RW_WIDTH) * lp['rw_gn_w'] + lp['rw_gn_b']
    bonus = jnp.sum(heads(r * k * lp['rw_r_k']), axis=-1, keepdims=True) * heads(v)
    y = (o + bonus.reshape(B, T, RW_WIDTH)) * (jax.nn.sigmoid(zg) @ lp['rw_g2'])
    return y.astype(z.dtype), jnp.stack(finals, axis=1)

def conv_module(zc, lp):
    a, b = jnp.split(zc, 2, axis=-1)
    u = a * jax.nn.sigmoid(b)
    u = lax.conv_general_dilated(
        u, lp['conv_w'][:, None, :], window_strides=(1,),
        padding=[(CONV_KERNEL // 2, CONV_KERNEL // 2)],
        dimension_numbers=('NWC', 'WIO', 'NWC'),
        feature_group_count=CONV_WIDTH) + lp['conv_b']
    return jax.nn.silu(layer_norm(u, lp['conv_ln_w'], lp['conv_ln_b']))

def rope_2d_tables(T):
    rows = T // GRID_W
    row, col = jnp.meshgrid(jnp.arange(rows), jnp.arange(GRID_W), indexing='ij')
    inv = ROPE_THETA ** (-jnp.arange(0, ROT_HALF, 2, dtype=jnp.float32) / ROT_HALF)
    ang_r = row.reshape(-1, 1).astype(jnp.float32) * inv
    ang_c = col.reshape(-1, 1).astype(jnp.float32) * inv
    return jnp.cos(ang_r), jnp.sin(ang_r), jnp.cos(ang_c), jnp.sin(ang_c)

def _rotate(x, cos, sin):
    x1, x2 = jnp.split(x, 2, axis=-1)
    cos = cos[:, None, :]
    sin = sin[:, None, :]
    return jnp.concatenate([x1 * cos - x2 * sin, x1 * sin + x2 * cos], axis=-1)

def apply_rope_2d(x, tabs):
    cr, sr, cc, sc = tabs
    xr, xc = jnp.split(x, 2, axis=-1)
    return jnp.concatenate([_rotate(xr, cr, sr), _rotate(xc, cc, sc)], axis=-1).astype(x.dtype)

def block_attention(q, k, v):
    B, Tq = q.shape[:2]
    nb = Tq // Q_BLOCK
    qb = jnp.moveaxis(q.reshape(B, nb, Q_BLOCK, ATT_KV_HEADS, ATT_GROUP, HEAD_DIM), 1, 0)
    scale = HEAD_DIM ** -0.5

    def one_block(q_blk):
        s = jnp.einsum('bqhgd,bkhd->bhgqk', q_blk, k).astype(jnp.float32) * scale
        p = jax.nn.softmax(s, axis=-1)
        return jnp.einsum('bhgqk,bkhd->bqhgd', p.astype(v.dtype), v)

    out = lax.map(one_block, qb)
    return jnp.moveaxis(out, 0, 1).reshape(B, Tq, ATT_HEADS * HEAD_DIM)

def peer_ffn(h, lp):
    B, T, D = h.shape
    u_tab, v_tab, sub_keys, wq = lp['peer_u'], lp['peer_v'], lp['peer_keys'], lp['peer_wq']

    def chunk(hx):
        C = hx.shape[0]
        q = (hx @ wq).reshape(C, PEER_HEADS, 2, PEER_HALF)
        s = jnp.einsum('chpd,hpkd->chpk', q, sub_keys).astype(jnp.float32)
        sv, si = lax.top_k(s, PEER_TOPK)
        comb = (sv[:, :, 0, :, None] + sv[:, :, 1, None, :]).reshape(C, PEER_HEADS, PEER_TOPK * PEER_TOPK)
        fv, fi = lax.top_k(comb, PEER_TOPK)
        e1 = jnp.take_along_axis(si[:, :, 0], fi // PEER_TOPK, axis=-1)
        e2 = jnp.take_along_axis(si[:, :, 1], fi % PEER_TOPK, axis=-1)
        idx = e1 * PEER_N_KEYS + e2
        g = jax.nn.softmax(fv, axis=-1)
        u = jnp.take(u_tab, idx, axis=0)
        act = jax.nn.gelu(jnp.einsum('chkd,cd->chk', u, hx).astype(jnp.float32), approximate=False)
        vv = jnp.take(v_tab, idx, axis=0)
        return jnp.einsum('chk,chkd->cd', (g * act).astype(hx.dtype), vv)

    return lax.map(chunk, h.reshape(-1, PEER_CHUNK, D)).reshape(B, T, D)

def trunk_layer(x, mod, lp, is_latent, ctx_k, ctx_v, s0):
    shift1, scale1, gate1, shift2, scale2, gate2 = mod
    B, T, _ = x.shape
    h = modulate(x, shift1, scale1)
    z = h @ lp['w_in']
    z_rw, z_cv, z_q, z_k, z_v, z_gate = _split(z, IN_SIZES)
    y_rw, s_fin = rwkv_mixer(z_rw, lp, s0)
    y_cv = conv_module(z_cv, lp)
    q = head_rms_norm(z_q.reshape(B, T, ATT_HEADS, HEAD_DIM), lp['q_norm'])
    k = head_rms_norm(z_k.reshape(B, T, ATT_KV_HEADS, HEAD_DIM), lp['k_norm'])
    v = z_v.reshape(B, T, ATT_KV_HEADS, HEAD_DIM)
    if is_latent:
        tabs = rope_2d_tables(T)
        q = apply_rope_2d(q, tabs)
        k = apply_rope_2d(k, tabs)
        keys = jnp.concatenate([k, ctx_k.astype(k.dtype)], axis=1)
        vals = jnp.concatenate([v, ctx_v.astype(v.dtype)], axis=1)
    else:
        keys, vals = k, v
    y_at = block_attention(q.reshape(B, T, ATT_KV_HEADS, ATT_GROUP, HEAD_DIM), keys, vals)
    g_a, g_b, g_c = jnp.split(jax.nn.sigmoid(z_gate), N_BRANCH, axis=-1)
    merged = (g_a * (y_rw @ lp['w_out_rwkv'])
              + g_b * (y_cv @ lp['w_out_conv'])
              + g_c * (y_at @ lp['w_out_attn']))
    x = x + gate1 * (merged @ lp['w_o'])
    x = x + gate2 * peer_ffn(modulate(x, shift2, scale2), lp)
    return x, k, v, s_fin

def setup_inputs(seed: int = 0) -> dict:
    key = jax.random.key(seed)
    ks = iter(jax.random.split(key, 40))
    L, D = DEPTH, D_MODEL
    f32 = jnp.float32

    def nrm(shape, scale):
        return jax.random.normal(next(ks), shape, f32) * scale

    def near_one(shape):
        return 1.0 + nrm(shape, 0.1)

    return {
        'x_prompt': nrm((BATCH, SEQ, D), 1.0),
        'x_sample': nrm((DEC_BATCH, DEC_SEQ, D), 1.0),
        'c': nrm((DEC_BATCH, D), 1.0),
        'cache_k': nrm((DEC_BATCH, L, PAST_LEN, ATT_KV_HEADS, HEAD_DIM), 1.0),
        'cache_v': nrm((DEC_BATCH, L, PAST_LEN, ATT_KV_HEADS, HEAD_DIM), 1.0),
        'state_wkv': nrm((DEC_BATCH, L, 2, RW_HEADS, RW_HEAD_DIM, RW_HEAD_DIM), 0.5),
        'c_ctx': nrm((D,), 1.0),
        'w_mod': nrm((L, D, N_MOD * D), 0.5 * D ** -0.5),
        'b_mod': nrm((L, N_MOD * D), 0.02),
        'w_in': nrm((L, D, IN_COLS), D ** -0.5),
        'shift_mu_prev': 0.25 + nrm((L, RW_COLS), 0.05),
        'shift_mu_next': 0.25 + nrm((L, RW_COLS), 0.05),
        'rw_w0': jax.random.uniform(next(ks), (L, 2, RW_WIDTH), f32, -4.0, 0.0),
        'rw_w2': nrm((L, 2, RW_LORA_W, RW_WIDTH), 0.1 * RW_LORA_W ** -0.5),
        'rw_a0': nrm((L, 2, RW_WIDTH), 0.1),
        'rw_a2': nrm((L, 2, RW_LORA_A, RW_WIDTH), 0.5 * RW_LORA_A ** -0.5),
        'rw_g2': nrm((L, RW_LORA_G, RW_WIDTH), RW_LORA_G ** -0.5),
        'rw_k_k': near_one((L, RW_WIDTH)),
        'rw_k_a': near_one((L, RW_WIDTH)),
        'rw_r_k': nrm((L, RW_WIDTH), 0.1),
        'rw_gn_w': near_one((L, RW_WIDTH)),
        'rw_gn_b': nrm((L, RW_WIDTH), 0.02),
        'w_out_rwkv': nrm((L, RW_WIDTH, D), RW_WIDTH ** -0.5),
        'conv_w': nrm((L, CONV_KERNEL, CONV_WIDTH), CONV_KERNEL ** -0.5),
        'conv_b': nrm((L, CONV_WIDTH), 0.02),
        'conv_ln_w': near_one((L, CONV_WIDTH)),
        'conv_ln_b': nrm((L, CONV_WIDTH), 0.02),
        'w_out_conv': nrm((L, CONV_WIDTH, D), CONV_WIDTH ** -0.5),
        'q_norm': near_one((L, HEAD_DIM)),
        'k_norm': near_one((L, HEAD_DIM)),
        'w_out_attn': nrm((L, ATT_HEADS * HEAD_DIM, D), (ATT_HEADS * HEAD_DIM) ** -0.5),
        'w_o': nrm((L, D, D), D ** -0.5),
        'peer_wq': nrm((L, D, PEER_HEADS * PEER_KEY_DIM), D ** -0.5),
        'peer_keys': nrm((L, PEER_HEADS, 2, PEER_N_KEYS, PEER_HALF), PEER_HALF ** -0.5),
        'peer_u': nrm((L, PEER_N_EXPERTS, D), D ** -0.5),
        'peer_v': nrm((L, PEER_N_EXPERTS, D), PEER_HEADS ** -0.5),
    }

def reference(x_prompt, x_sample, c, cache_k, cache_v, state_wkv, c_ctx, w_mod, b_mod, w_in,
              shift_mu_prev, shift_mu_next, rw_w0, rw_w2, rw_a0, rw_a2, rw_g2, rw_k_k, rw_k_a,
              rw_r_k, rw_gn_w, rw_gn_b, w_out_rwkv, conv_w, conv_b, conv_ln_w, conv_ln_b,
              w_out_conv, q_norm, k_norm, w_out_attn, w_o, peer_wq, peer_keys, peer_u, peer_v):
    xp, xs = x_prompt, x_sample
    n_req = xp.shape[0]
    ctx_k, ctx_v, ctx_s = [], [], []
    for l in range(DEPTH):
        lp = dict(
            w_in=w_in[l], shift_mu_prev=shift_mu_prev[l], shift_mu_next=shift_mu_next[l],
            rw_w0=rw_w0[l], rw_w2=rw_w2[l], rw_a0=rw_a0[l], rw_a2=rw_a2[l], rw_g2=rw_g2[l],
            rw_k_k=rw_k_k[l], rw_k_a=rw_k_a[l], rw_r_k=rw_r_k[l], rw_gn_w=rw_gn_w[l],
            rw_gn_b=rw_gn_b[l], w_out_rwkv=w_out_rwkv[l], conv_w=conv_w[l], conv_b=conv_b[l],
            conv_ln_w=conv_ln_w[l], conv_ln_b=conv_ln_b[l], w_out_conv=w_out_conv[l],
            q_norm=q_norm[l], k_norm=k_norm[l], w_out_attn=w_out_attn[l], w_o=w_o[l],
            peer_wq=peer_wq[l], peer_keys=peer_keys[l], peer_u=peer_u[l], peer_v=peer_v[l])
        zero_state = jnp.zeros((n_req, 2, RW_HEADS, RW_HEAD_DIM, RW_HEAD_DIM), jnp.float32)
        mod_ctx = modulation(c_ctx, w_mod[l], b_mod[l])
        xp, k_l, v_l, s_l = trunk_layer(xp, mod_ctx, lp, False, None, None, zero_state)
        ctx_k.append(k_l)
        ctx_v.append(v_l)
        ctx_s.append(s_l)
        mod_lat = modulation(c[:, None, :], w_mod[l], b_mod[l])
        xs, _, _, _ = trunk_layer(xs, mod_lat, lp, True, cache_k[:, l], cache_v[:, l], state_wkv[:, l])
    new_cache_k = jnp.stack(ctx_k, axis=1)
    new_cache_v = jnp.stack(ctx_v, axis=1)
    new_state_wkv = jnp.stack(ctx_s, axis=1)
    return (xp, xs, new_cache_k, new_cache_v, new_state_wkv)


_drawn_inputs = setup_inputs


def setup_inputs(seed=0):
    import zlib

    import numpy as np

    out = dict(_drawn_inputs(seed))
    spreads = {}
    factors = {'cache_k': 6.005,
     'cache_v': 5.176,
     'state_wkv': 4.083,
     'rw_w2': 3.885,
     'rw_gn_w': 3.853,
     'rw_gn_b': 8.0,
     'conv_b': 6.918,
     'conv_ln_w': 2.74,
     'conv_ln_b': 8.0,
     'q_norm': 8.0}
    for name, (base, spread) in spreads.items():
        noise = np.random.default_rng([zlib.crc32(name.encode()), seed]).standard_normal(out[name].shape)
        drawn = base * np.exp(spread * noise) if base else spread * noise
        out[name] = __import__('jax').numpy.asarray(drawn.astype(out[name].dtype))
    for name, factor in factors.items():
        out[name] = (out[name] * factor).astype(out[name].dtype)
    return out
```

```python
from contextlib import ExitStack

import numpy as np
import concourse.bass as bass
from concourse import mybir

F32 = mybir.dt.float32
U32 = mybir.dt.uint32
ALU = mybir.AluOpType
ACT = mybir.ActivationFunctionType
AX = mybir.AxisListType.X
ds = bass.ds

P = 128
D = 1024
KD = D // P
DEPTH = 2
CTX, LAT = 128, 512
NTOK = CTX + LAT
TILES = NTOK // P
NMOD = 6
W = 512
HD = 64
HEADS = 8
PAIRS = HEADS // 2
RW_COLS = 1920
COL_LORA, COL_CONV, COL_Q, COL_KV, COL_GATE = 1536, 1920, 2944, 3456, 3712
IN_COLS = 6784
TAPS = 31
HALF_TAPS = TAPS // 2
EXPERTS, KEYS, TOPK = 16384, 128, 16
RMS_EPS, LN_EPS, GN_EPS, KK_EPS = 1e-6, 1e-5, 64e-5, 1e-12
DECAY_SCALE = -float(np.exp(-0.5))
CORE_ROWS = P + 2
GROUPS = ((0, CTX), (CTX, LAT))
LORA_PAD = (1, CTX + 2)
LORA_W = NTOK + 3
CONV_PAD = (HALF_TAPS, CTX + 2 * HALF_TAPS)
CONV_W = NTOK + 3 * HALF_TAPS
CONV_SPAN = CONV_W - 2 * HALF_TAPS


class Tensors:

    def __init__(self, dram):
        self.dram = dram


class Steps:

    def __init__(self, engine, semaphore, base=0):
        self.engine, self.semaphore, self.base, self.n = engine, semaphore, base, 0

    def mark(self, instruction):
        self.n += 1
        instruction.then_inc(self.semaphore, 1)

    def step(self, instruction):
        self.mark(instruction)
        self.engine.wait_ge(self.semaphore, self.base + self.n)

    def wait_all(self):
        self.engine.wait_ge(self.semaphore, self.base + self.n)


class Marks:

    def __init__(self, *names):
        self.names = names

    def after(self, name, turn=0):
        return turn * len(self.names) + self.names.index(name) + 1

    def all(self, turns):
        return turns * len(self.names)


def each_tile(engine, tile):
    tile(0, False)
    with engine.Fori(1, TILES) as i:
        tile(i, True)


def stage_semaphores(nc, stack):
    banks = [[stack.enter_context(nc.semaphore(f"bank{b}_{k}"))
              for k in range(max(len(names) for _, names in STAGES[b::2]))] for b in range(2)]
    stages = {name: dict(zip(names, banks[n % 2])) for n, (name, names) in enumerate(STAGES)}
    for name, names in OUTER_STAGES:
        stages[name] = {n: stack.enter_context(nc.semaphore(f"{name}_{n}")) for n in names}
    return stages


def clear(engine, before):
    engine.dma_reset()
    for semaphore in before.values():
        engine.sem_clear(semaphore)


def modulation_stage(nc, t, s, before, layer):
    with ExitStack() as mem:
        weights = [mem.enter_context(nc.sbuf_tensor(f"modulation_weights{b}", [P, KD, 512], F32)) for b in range(2)]
        sig = mem.enter_context(nc.sbuf_tensor("cond_sigmoid", [P, KD, 2], F32))
        silu = mem.enter_context(nc.sbuf_tensor("cond_silu", [P, KD, 2], F32))
        bias = mem.enter_context(nc.sbuf_tensor("modulation_bias", [P, NMOD * KD], F32))
        diag = [mem.enter_context(nc.sbuf_tensor(f"gate_diagonal{b}", [P, 4, P], F32)) for b in range(2)]
        product = [t.bank[b][:, 0:8].rearrange("p (j c) -> p j c", c=2) for b in range(2)]
        row = t.bank[2:4]
        block = mem.enter_context(nc.Block())
        chunks = NMOD * D // 512

        @block.sync
        def _(sp):
            sp.dma_start(bias[:, :], t.dram["b_mod"][layer, :, :]).then_inc(s["bias_loaded"], 16)
            with sp.Fori(0, chunks // 2) as i:
                for b in range(2):
                    sp.wait_ge(s["free0"] if b == 0 else s["free1"], i + 1)
                    sp.dma_start(weights[b][:, :, :],
                                 t.dram["w_mod"][layer, :, :].rearrange("(k p) n -> p k n", p=P)[:, :, ds((i * 2 + b) * 512, 512)]
                                 ).then_inc(s["loaded0"] if b == 0 else s["loaded1"], 16)

        @block.gpsimd
        def _(pool):
            clear(pool, before)

        @block.scalar
        def _(act):
            nc.scalar.activation(sig[:, :, :], t.cond[:, :, :], ACT.Sigmoid).then_inc(s["sigmoid"], 1)
            for g in range(8):
                act.wait_ge(s["row_product"], g + 1)
                gate, c, half = g // 4, g // 2 % 2, g % 2
                nc.scalar.copy(t.gate_rows[:, gate, c, half * 512:half * 512 + 512], row[g % 2][:, :]).then_inc(s["row_copied"], 1)

        @block.tensor
        def _(pe):
            pe.sem_inc(s["free0"], 1)
            pe.sem_inc(s["free1"], 1)
            pe.wait_ge(s["silu"], 1)
            with pe.Fori(0, chunks // 2) as i:
                for b in range(2):
                    pe.wait_ge(s["loaded0"] if b == 0 else s["loaded1"], (i + 1) * 16)
                    pe.wait_ge(s["psum_free"], i * 2 + b + 1)
                    for j in range(4):
                        for k in range(KD):
                            last = nc.tensor.matmul(product[b][:, j, :], weights[b][:, k, j * P:(j + 1) * P],
                                                    silu[:, k, :], start=(k == 0), stop=(k == KD - 1))
                    last.then_inc(s["free0"] if b == 0 else s["free1"], 1)
            for g in range(8):
                pe.wait_ge(s["diagonal"], g + 1)
                if g >= 2:
                    pe.wait_ge(s["row_copied"], g - 1)
                nc.tensor.matmul(row[g % 2][:, :], t.ones[:, :], diag[g % 2][:, :, :].rearrange("p a b -> p (a b)"),
                                 start=True, stop=True).then_inc(s["row_product"], 1)

        @block.vector
        def _(dve):
            dve.wait_ge(s["sigmoid"], 1)
            nc.vector.tensor_tensor(silu[:, :, :], t.cond[:, :, :], sig[:, :, :], ALU.mult).then_inc(s["silu"], 1)
            dve.sem_inc(s["psum_free"], 2)
            dve.wait_ge(s["bias_loaded"], 16)
            with dve.Fori(0, chunks // 2) as i:
                for b in range(2):
                    dve.wait_ge(s["free0"] if b == 0 else s["free1"], i + 2)
                    at = (i * 2 + b) * 4
                    nc.vector.tensor_tensor(t.mod[:, ds(at, 4), :], product[b][:, :, :],
                                            bias[:, ds(at, 4)].unsqueeze(2).to_broadcast([P, 4, 2]),
                                            ALU.add).then_inc(s["psum_free"], 1)
            dve.wait_ge(s["psum_free"], 2 + chunks)
            done = Steps(dve, s["vector_steps"])
            for which in (1, 4):
                v = t.mod[:, which * KD:(which + 1) * KD, :]
                done.mark(nc.vector.tensor_scalar(v, v, 1.0, None, ALU.add))
            for g in range(8):
                gate, c, half = g // 4, g // 2 % 2, g % 2
                at = (2 + 3 * gate) * KD + half * 4
                if g >= 2:
                    dve.wait_ge(s["row_product"], g - 1)
                nc.vector.tensor_tensor(diag[g % 2][:, :, :], t.ident[:, :].unsqueeze(1).to_broadcast([P, 4, P]),
                                        t.mod[:, at:at + 4, c:c + 1].to_broadcast([P, 4, P]), ALU.mult
                                        ).then_inc(s["diagonal"], 1)
            done.wait_all()


MODULATION = ("bias_loaded", "free0", "free1", "loaded0", "loaded1", "sigmoid", "silu", "psum_free",
              "row_product", "row_copied", "diagonal", "vector_steps")


def norm_stage(nc, t, s, before, which):
    with ExitStack() as mem:
        square = mem.enter_context(nc.sbuf_tensor(f"square{which}", [P, D], F32))
        total = mem.enter_context(nc.sbuf_tensor(f"square_sum{which}", [P, TILES], F32))
        root = mem.enter_context(nc.sbuf_tensor(f"rms_root{which}", [P, TILES], F32))
        inverse = mem.enter_context(nc.sbuf_tensor(f"rms_inverse{which}", [P, TILES], F32))
        normed = [mem.enter_context(nc.sbuf_tensor(f"normed{which}_{b}", [P, D], F32)) for b in range(2)]
        turned = t.bank[0:4]
        block = mem.enter_context(nc.Block())

        @block.gpsimd
        def _(pool):
            clear(pool, before)

        @block.scalar
        def _(act):
            for i in range(TILES):
                if i:
                    act.wait_ge(s["squared"], i)
                nc.scalar.activation(square[:, :], t.x[:, i, :], ACT.Square, accum_out=total[:, i:i + 1]).then_inc(s["squared"], 1)
            act.wait_ge(s["mean"], 1)
            nc.scalar.activation(root[:, :], total[:, :], ACT.Sqrt).then_inc(s["root"], 1)
            for i in range(TILES):
                act.wait_ge(s["turned"], 2 * i + 2)
                for k in range(4):
                    last = nc.scalar.activation(t.h[:, 4 + k, i * P:(i + 1) * P], turned[2 * (i % 2) + 1][:, k * P:(k + 1) * P],
                                                ACT.Identity, bias=t.mod[:, which * KD + 4 + k, min(i, 1):min(i, 1) + 1],
                                                scale=t.mod[:, (which + 1) * KD + 4 + k, min(i, 1):min(i, 1) + 1])
                last.then_inc(s["scalar_wrote"], 1)
            act.wait_ge(s["scalar_wrote"], TILES)

        @block.tensor
        def _(pe):
            for i in range(TILES):
                pe.wait_ge(s["normed"], i + 1)
                for half in range(2):
                    if i >= 2:
                        pe.wait_ge(s["scalar_wrote"] if half else s["vector_wrote"], i - 1)
                    for k in range(4):
                        last = nc.tensor.transpose(turned[2 * (i % 2) + half][:, k * P:(k + 1) * P],
                                                   normed[i % 2][:, (half * 4 + k) * P:(half * 4 + k + 1) * P], t.ident[:, :])
                    last.then_inc(s["turned"], 1)

        @block.vector
        def _(dve):
            dve.wait_ge(s["squared"], TILES)
            nc.vector.tensor_scalar(total[:, :], total[:, :], 1.0 / D, RMS_EPS, ALU.mult, ALU.add).then_inc(s["mean"], 1)
            dve.wait_ge(s["root"], 1)
            nc.vector.reciprocal(inverse[:, :], root[:, :]).then_inc(s["inverse"], 1)
            dve.wait_ge(s["inverse"], 1)

            def modulate(i):
                dve.wait_ge(s["turned"], 2 * i + 1)
                for k in range(4):
                    last = nc.vector.tensor_scalar(t.h[:, k, i * P:(i + 1) * P], turned[2 * (i % 2)][:, k * P:(k + 1) * P],
                                                   t.mod[:, (which + 1) * KD + k, min(i, 1):min(i, 1) + 1],
                                                   t.mod[:, which * KD + k, min(i, 1):min(i, 1) + 1], ALU.mult, ALU.add)
                last.then_inc(s["vector_wrote"], 1)

            for i in range(TILES):
                if i >= 2:
                    dve.wait_ge(s["turned"], 2 * (i - 1))
                nc.vector.tensor_scalar(normed[i % 2][:, :], t.x[:, i, :], inverse[:, i:i + 1], None, ALU.mult
                                        ).then_inc(s["normed"], 1)
                if i:
                    modulate(i - 1)
            modulate(TILES - 1)
            dve.wait_ge(s["vector_wrote"], TILES)


NORM = ("squared", "mean", "root", "turned", "scalar_wrote", "normed", "vector_wrote", "inverse")


def project_stage(nc, t, s, before, layer):
    with ExitStack() as mem:
        weights = [mem.enter_context(nc.sbuf_tensor(f"in_weights{b}", [P, KD, 512], F32)) for b in range(2)]
        staged = [mem.enter_context(nc.sbuf_tensor(f"rkv_staged{b}", [P, 512], F32)) for b in range(4)]
        conv_a = mem.enter_context(nc.sbuf_tensor("conv_a", [P, 4, NTOK], F32))
        gate = [mem.enter_context(nc.sbuf_tensor(f"conv_gate{b}", [P, 512], F32)) for b in range(2)]
        zero = mem.enter_context(nc.sbuf_tensor("zero_row", [1, 3 * W], F32))
        acc = t.bank
        block = mem.enter_context(nc.Block())
        chunks = ((0, 512), (512, 512), (1024, 512), (COL_Q, 512), (COL_KV, 256), (COL_LORA, 384), (COL_CONV, 512), (COL_CONV + 512, 512))
        units = [(c, i, None) for c in range(5) for i in range(TILES)]
        units += [(c, j, g) for c in range(5, 8) for j in range(chunks[c][1] // P) for g in range(2)]
        last_of_chunk = {c: max(n for n, u in enumerate(units) if u[0] == c) for c in range(8)}
        by_scalar = [n for n, (c, _, _) in enumerate(units) if c == 7 or n % 2 == 0]
        by_vector = [n for n in range(len(units)) if n not in by_scalar]

        def emptied(engine, n):
            if n in by_scalar:
                engine.wait_ge(s["scalar_emptied"], by_scalar.index(n) + 1)
            else:
                engine.wait_ge(s["vector_emptied"], by_vector.index(n) + 1)

        def target(n):
            c, i, g = units[n]
            if c < 3:
                return staged[n % 4][:, :]
            if c < 5:
                return t.qkv[:, i, (c - 3) * 512:(c - 3) * 512 + chunks[c][1]]
            lo, m = GROUPS[g]
            if c == 5:
                return t.lora[:, i, LORA_PAD[g]:LORA_PAD[g] + m]
            if c == 6:
                return conv_a[:, i, lo:lo + m]
            return gate[n % 2][:, 0:m]

        def width(n):
            c, i, g = units[n]
            return chunks[c][1] if g is None else GROUPS[g][1]

        def stored_by(n, b):
            return sum(16 * (1 + (units[m][1] in (1, 2, 3)) + (units[m][1] in (2, 3, 4))) for m in range(b, n, 4))

        def stage_free(engine, n):
            if 4 <= n < 3 * TILES:
                engine.wait_ge((s["stored0"], s["stored1"], s["stored2"], s["stored3"])[n % 4], stored_by(n, n % 4))

        @block.sync
        def _(sp):
            for c, (at, m) in enumerate(chunks):
                if c >= 2:
                    sp.wait_ge(s["product"], last_of_chunk[c - 2] + 1)
                sp.dma_start(weights[c % 2][:, :, 0:m],
                             t.dram["w_in"][layer, :, at:at + m].rearrange("(k p) n -> p k n", p=P)
                             ).then_inc(s["loaded0"] if c % 2 == 0 else s["loaded1"], 16)

        @block.gpsimd
        def _(pool):
            clear(pool, before)
            nc.gpsimd.memset(zero[:, :], 0.0).then_inc(s["zeroed"], 1)
            pool.wait_ge(s["zeroed"], 1)
            for row in (0, CORE_ROWS - 1, CORE_ROWS, TILES * CORE_ROWS - 1):
                nc.gpsimd.dma_start(t.dram["rkv_scratch"][row:row + 1, :], zero[:, :]).then_inc(s["zero_stored"], 16)
            for n in range(3 * TILES):
                c, i, _ = units[n]
                cols = slice(c * 512, c * 512 + 512)
                emptied(pool, n)
                buffer_stored = (s["stored0"], s["stored1"], s["stored2"], s["stored3"])[n % 4]
                nc.gpsimd.dma_start(t.dram["rkv_scratch"][i * CORE_ROWS + 1:i * CORE_ROWS + 1 + P, cols], staged[n % 4][:, :]
                                    ).then_inc(buffer_stored, 16)
                up = i in (1, 2, 3)
                down = i in (2, 3, 4)
                if up:
                    nc.gpsimd.dma_start(t.dram["rkv_scratch"][(i + 1) * CORE_ROWS:(i + 1) * CORE_ROWS + 1, cols],
                                        staged[n % 4][P - 1:P, :]).then_inc(buffer_stored, 16)
                if down:
                    nc.gpsimd.dma_start(t.dram["rkv_scratch"][i * CORE_ROWS - 1:i * CORE_ROWS, cols],
                                        staged[n % 4][0:1, :]).then_inc(buffer_stored, 16)
            for b in range(4):
                pool.wait_ge((s["stored0"], s["stored1"], s["stored2"], s["stored3"])[b], stored_by(3 * TILES, b))
            pool.wait_ge(s["zero_stored"], 64)

        @block.tensor
        def _(pe):
            for n, (c, i, g) in enumerate(units):
                if n == 0 or units[n - 1][0] != c:
                    pe.wait_ge(s["loaded0"] if c % 2 == 0 else s["loaded1"], 16 * (c // 2 + 1))
                if n >= 8:
                    emptied(pe, n - 8)
                for k in range(KD):
                    if g is None:
                        last = nc.tensor.matmul(acc[n % 8][:, 0:width(n)], t.h[:, k, i * P:(i + 1) * P],
                                                weights[c % 2][:, k, 0:chunks[c][1]], start=(k == 0), stop=(k == KD - 1))
                    else:
                        lo, m = GROUPS[g]
                        last = nc.tensor.matmul(acc[n % 8][:, 0:m], weights[c % 2][:, k, i * P:(i + 1) * P],
                                                t.h[:, k, lo:lo + m], start=(k == 0), stop=(k == KD - 1))
                last.then_inc(s["product"], 1)

        @block.scalar
        def _(act):
            for n in by_scalar:
                act.wait_ge(s["product"], n + 1)
                stage_free(act, n)
                if units[n][0] == 7:
                    if n - last_of_chunk[6] > 2:
                        act.wait_ge(s["gated"], n - last_of_chunk[6] - 2)
                    nc.scalar.activation(target(n), acc[n % 8][:, 0:width(n)], ACT.Sigmoid).then_inc(s["scalar_emptied"], 1)
                else:
                    nc.scalar.copy(target(n), acc[n % 8][:, 0:width(n)]).then_inc(s["scalar_emptied"], 1)
            act.wait_ge(s["scalar_emptied"], len(by_scalar))

        @block.vector
        def _(dve):
            for at in (0, CTX + 1, LORA_W - 1):
                nc.vector.memset(t.lora[:, :, at:at + 1], 0.0).then_inc(s["padded"], 1)
            for at in (0, HALF_TAPS + CTX, CONV_W - HALF_TAPS):
                nc.vector.memset(t.conv_in[:, :, at:at + HALF_TAPS], 0.0).then_inc(s["padded"], 1)
            for n in by_vector:
                dve.wait_ge(s["product"], n + 1)
                stage_free(dve, n)
                nc.vector.tensor_copy(target(n), acc[n % 8][:, 0:width(n)]).then_inc(s["vector_emptied"], 1)
            dve.wait_ge(s["vector_emptied"], len(by_vector))
            for n in range(last_of_chunk[6] + 1, len(units)):
                _, j, g = units[n]
                lo, m = GROUPS[g]
                emptied(dve, n)
                nc.vector.tensor_tensor(t.conv_in[:, j, CONV_PAD[g]:CONV_PAD[g] + m], conv_a[:, j, lo:lo + m],
                                        gate[n % 2][:, 0:m], ALU.mult).then_inc(s["gated"], 1)
            dve.wait_ge(s["gated"], 8)
            dve.wait_ge(s["padded"], 6)


PROJECT = ("loaded0", "loaded1", "product", "scalar_emptied", "vector_emptied", "zeroed", "zero_stored",
           "stored0", "stored1", "stored2", "stored3", "gated", "padded")


def conv_stage(nc, t, s, before, layer):
    with ExitStack() as mem:
        def sbuf(name, *shape):
            return mem.enter_context(nc.sbuf_tensor("conv_" + name, [P, *shape], F32))

        taps, rows = sbuf("taps", 4, TAPS), sbuf("rows", 3, 4)
        acc, centred, square = sbuf("acc", 4, CONV_SPAN), sbuf("centred", 4, NTOK), sbuf("square", 4, NTOK)
        variance, inverse = sbuf("variance", NTOK), sbuf("inverse", NTOK)
        mean_bank, var_bank = t.bank[0:2], t.bank[2:4]
        block = mem.enter_context(nc.Block())

        def span(g):
            return CONV_PAD[g] - HALF_TAPS, GROUPS[g][1]

        @block.sync
        def _(sp):
            sp.dma_start(taps[:, :, :], t.dram["conv_taps"][layer, :, :, :]).then_inc(s["loaded"], 16)
            sp.dma_start(rows[:, :, :], t.dram["conv_rows"][layer, :, :, :]).then_inc(s["loaded"], 16)

        @block.gpsimd
        def _(pool):
            clear(pool, before)

        @block.tensor
        def _(pe):
            pe.wait_ge(s["convolved"], 4 * TAPS)
            for g in range(2):
                at, m = span(g)
                for j in range(4):
                    last = nc.tensor.matmul(mean_bank[g][:, 0:m], t.ones[:, :], acc[:, j, at:at + m], start=(j == 0), stop=(j == 3))
                last.then_inc(s["mean"], 1)
            for g, (lo, m) in enumerate(GROUPS):
                pe.wait_ge(s["squared"], g + 1)
                for j in range(4):
                    last = nc.tensor.matmul(var_bank[g][:, 0:m], t.ones[:, :], square[:, j, lo:lo + m], start=(j == 0), stop=(j == 3))
                last.then_inc(s["variance"], 1)

        @block.scalar
        def _(act):
            for g, (lo, m) in enumerate(GROUPS):
                act.wait_ge(s["centred"], g + 1)
                nc.scalar.activation(square[:, :, lo:lo + m], centred[:, :, lo:lo + m], ACT.Square).then_inc(s["squared"], 1)
            act.wait_ge(s["with_eps"], 2)
            nc.scalar.activation(variance[:, :], variance[:, :], ACT.Sqrt).then_inc(s["root"], 1)
            act.wait_ge(s["scaled"], 4)
            nc.scalar.activation(square[:, :, :], centred[:, :, :], ACT.Sigmoid).then_inc(s["sigmoid"], 1)

        @block.vector
        def _(dve):
            dve.wait_ge(s["loaded"], 32)
            with dve.Fori(0, 4) as j:
                done = Steps(dve, s["convolved"], j * TAPS)
                out = acc[:, ds(j, 1), :]
                done.step(nc.vector.tensor_scalar(out, t.conv_in[:, ds(j, 1), 0:CONV_SPAN], taps[:, ds(j, 1), 0:1], rows[:, 0:1, ds(j, 1)],
                                                  ALU.mult, ALU.add))
                for k in range(1, TAPS):
                    done.step(nc.vector.scalar_tensor_tensor(out=out, in0=t.conv_in[:, ds(j, 1), k:k + CONV_SPAN],
                                                             scalar=taps[:, ds(j, 1), k:k + 1], in1=out, op0=ALU.mult, op1=ALU.add))
            for g, (lo, m) in enumerate(GROUPS):
                dve.wait_ge(s["mean"], g + 1)
                at, _ = span(g)
                nc.vector.scalar_tensor_tensor(out=centred[:, :, lo:lo + m], in0=mean_bank[g][:, 0:m].unsqueeze(1).to_broadcast([P, 4, m]),
                                               scalar=-1.0 / W, in1=acc[:, :, at:at + m], op0=ALU.mult, op1=ALU.add).then_inc(s["centred"], 1)
            for g, (lo, m) in enumerate(GROUPS):
                dve.wait_ge(s["variance"], g + 1)
                nc.vector.tensor_scalar(variance[:, lo:lo + m], var_bank[g][:, 0:m], 1.0 / W, LN_EPS, ALU.mult, ALU.add
                                        ).then_inc(s["with_eps"], 1)
            dve.wait_ge(s["root"], 1)
            done = Steps(dve, s["vector_steps"])
            done.step(nc.vector.reciprocal(inverse[:, :], variance[:, :]))
            done.step(nc.vector.tensor_tensor(centred[:, :, :], centred[:, :, :], inverse[:, :].unsqueeze(1).to_broadcast([P, 4, NTOK]), ALU.mult))
            for j in range(4):
                nc.vector.tensor_scalar(centred[:, j, :], centred[:, j, :], rows[:, 1, j:j + 1], rows[:, 2, j:j + 1], ALU.mult, ALU.add
                                        ).then_inc(s["scaled"], 1)
            dve.wait_ge(s["scaled"], 4)
            dve.wait_ge(s["sigmoid"], 1)
            done.step(nc.vector.tensor_tensor(t.y_conv[:, :, :], centred[:, :, :], square[:, :, :], ALU.mult))


CONV = ("loaded", "convolved", "mean", "squared", "variance", "centred", "with_eps", "root", "scaled", "sigmoid", "vector_steps")


def qk_stage(nc, t, s, before, layer):
    with ExitStack() as mem:
        def sbuf(name, *shape):
            return mem.enter_context(nc.sbuf_tensor("qk_" + name, [P, *shape], F32))

        square = sbuf("square", TILES, 640)
        total, root, inverse = (sbuf(n, TILES * 10) for n in ("total", "root", "inverse"))
        gain, rope = sbuf("gain", 640), sbuf("rope", 4, 2, HD)
        rotated = sbuf("rotated", 640)
        keys = sbuf("keys", TILES + 1, 2, P)
        block = mem.enter_context(nc.Block())

        def heads(tensor):
            return tensor.rearrange("p (g e) -> p g e", e=HD)

        @block.sync
        def _(sp):
            sp.dma_start(gain[:, :], t.dram["qk_gain"][layer, 0, :].partition_broadcast(P)).then_inc(s["loaded"], 16)
            sp.dma_start(rope[:, :, :, :], t.dram["rope"].rearrange("(t p) (c e) -> p t c e", p=P, e=HD)).then_inc(s["loaded"], 16)
            sp.dma_start(t.cached_v[:, :], t.dram["cache_v"][layer, :, :]).then_inc(s["loaded"], 16)
            sp.dma_start(keys[:, TILES, 0, :], t.dram["cache_k"][layer, :, :]).then_inc(s["cache_loaded"], 16)
            sp.dma_start(t.dram["new_v"][layer, :, :], t.qkv[:, 0, 640:768]).then_inc(s["stored"], 16)
            sp.wait_ge(s["vector_steps"], 5)
            sp.dma_start(t.dram["new_k"][layer, :, :], t.qkv[:, 0, 512:640]).then_inc(s["stored"], 16)
            sp.wait_ge(s["stored"], 32)
            sp.wait_ge(s["loaded"], 48)

        @block.gpsimd
        def _(pool):
            clear(pool, before)

        @block.scalar
        def _(act):
            nc.scalar.activation(square[:, :, :], t.qkv[:, :, 0:640], ACT.Square).then_inc(s["squared"], 1)
            act.wait_ge(s["vector_steps"], 2)
            nc.scalar.activation(root[:, :], total[:, :], ACT.Sqrt).then_inc(s["root"], 1)
            for i in range(TILES + 1):
                act.wait_ge(s["turned"], i + 1)
                nc.scalar.copy(t.keys[:, :, i * P:(i + 1) * P],
                               t.bank[i % 2][:, 0:2 * P].rearrange("p (v n) -> p v n", v=2)).then_inc(s["copied"], 1)
            act.wait_ge(s["copied"], TILES + 1)

        @block.tensor
        def _(pe):
            for i in range(TILES + 1):
                pe.wait_ge(s["keys_ready"], 3 * (i + 1) if i < TILES else 3 * TILES + 2)
                if i >= 2:
                    pe.wait_ge(s["copied"], i - 1)
                for v in range(2):
                    last = nc.tensor.transpose(t.bank[i % 2][:, v * P:(v + 1) * P], keys[:, i, v, :], t.ident[:, :])
                last.then_inc(s["turned"], 1)

        @block.vector
        def _(dve):
            done = Steps(dve, s["vector_steps"])
            groups = total[:, :].rearrange("p (t g) -> p t g", t=TILES)
            dve.wait_ge(s["squared"], 1)
            done.step(nc.vector.tensor_reduce(groups, square[:, :, :].rearrange("p t (g e) -> p t g e", e=HD), AX, ALU.add))
            done.step(nc.vector.tensor_scalar(total[:, :], total[:, :], 1.0 / HD, RMS_EPS, ALU.mult, ALU.add))
            dve.wait_ge(s["root"], 1)
            done.step(nc.vector.reciprocal(inverse[:, :], root[:, :]))
            all_heads = t.qkv[:, :, 0:640].rearrange("p t (g e) -> p t g e", e=HD)
            done.step(nc.vector.tensor_tensor(all_heads, all_heads, inverse[:, :].rearrange("p (t g) -> p t g", t=TILES).unsqueeze(3)
                                              .to_broadcast([P, TILES, 10, HD]), ALU.mult))
            dve.wait_ge(s["loaded"], 48)
            done.step(nc.vector.tensor_tensor(t.qkv[:, :, 0:640], t.qkv[:, :, 0:640],
                                              gain[:, :].unsqueeze(1).to_broadcast([P, TILES, 640]), ALU.mult))
            dve.wait_ge(s["cache_loaded"], 16)
            for i in range(TILES + 1):
                if 0 < i < TILES:
                    x = t.qkv[:, i, 0:640]
                    halves = x.rearrange("p (g h c e) -> p g h c e", g=10, h=2, c=2)
                    out = rotated[:, :].rearrange("p (g h c e) -> p g h c e", g=10, h=2, c=2)
                    sin = rope[:, i - 1, 1, :].rearrange("p (h c e) -> p h c e", h=2, c=2)
                    for c in range(2):
                        done.step(nc.vector.tensor_tensor(out[:, :, :, c, :], halves[:, :, :, 1 - c, :],
                                                          sin[:, :, c, :].unsqueeze(1).to_broadcast([P, 10, 2, 16]), ALU.mult))
                    done.step(nc.vector.tensor_tensor(heads(x), heads(x), rope[:, i - 1, 0, :].unsqueeze(1).to_broadcast([P, 10, HD]), ALU.mult))
                    done.step(nc.vector.tensor_tensor(x, x, rotated[:, :], ALU.add))
                if i < TILES:
                    nc.vector.tensor_copy(keys[:, i, 0, :], t.qkv[:, i, 512:640]).then_inc(s["keys_ready"], 1)
                    own = t.qkv[:, i, 512:640]
                else:
                    own = keys[:, i, 0, :]
                for v in range(2):
                    nc.vector.tensor_copy(keys[:, i, 1, v * HD:(v + 1) * HD], own[:, (1 - v) * HD:(2 - v) * HD]).then_inc(s["keys_ready"], 1)
            dve.wait_ge(s["keys_ready"], 3 * TILES + 2)


QK = ("loaded", "cache_loaded", "stored", "squared", "root", "turned", "copied", "keys_ready", "vector_steps")


def attention_stage(nc, t, s, before):
    scale = HD ** -0.5
    NK = 5 * P
    tensor_order, vector_order, scalar_order = ["q_turned", "scores0", "scores1"], ["q_copied", "max0", "bias0", "max1", "bias1"], ["q_staged", "exp0"]
    for h in range(HEADS):
        ahead = h + 2 < HEADS
        tensor_order += [f"turned{h}"] + [f"scores{h + 2}"] * ahead + [f"mixed{h}"]
        vector_order += [f"copied{h}"] + [f"max{h + 2}", f"bias{h + 2}"] * ahead
        scalar_order += [f"exp{h + 1}"] * (h + 1 < HEADS) + [f"copied{h}"]
    TENSOR = Marks(*tensor_order, "y_turned")
    VECTOR = Marks(*vector_order, "inverse", "y", "y_copied")
    SCALAR = Marks(*scalar_order)
    with ExitStack() as mem:
        def sbuf(name, *shape):
            return mem.enter_context(nc.sbuf_tensor("attention_" + name, [P, *shape], F32))

        q, q_turned = sbuf("q", W), sbuf("q_turned", PAIRS, P)
        largest, bias, total, inverse = (sbuf(n, HEADS) for n in ("largest", "bias", "total", "inverse"))
        probs = [sbuf(f"probs{b}", NK) for b in range(2)]
        probs_turned = [sbuf(f"probs_turned{b}", NK) for b in range(2)]
        y, unused = sbuf("y", W), sbuf("unused", 1)
        block = mem.enter_context(nc.Block())
        scores_of = [t.psum[:, 2 * b:2 * b + 2, :].rearrange("p a n -> p (a n)") for b in range(2)]
        q_bank, turned_bank, turned_last, mixed_bank = t.bank[4], t.bank[5], t.bank[6], t.bank[7]

        @block.gpsimd
        def _(pool):
            clear(pool, before)

        @block.tensor
        def _(pe):
            def tile(i, latent):
                keys_blocks = 5 if latent else 1

                def scores(h):
                    if h >= 2:
                        pe.wait_ge(s["scalar"], SCALAR.after(f"exp{h - 2}", i))
                    b = HD * (h % 2)
                    v = 0 if h // 4 == h % 2 else 1
                    out, lhs = scores_of[h % 2], q_turned[b:b + HD, h // 2, :]
                    if latent:
                        nc.tensor.matmul(out[:, 0:512], lhs, t.keys[b:b + HD, v, P:5 * P], start=True, stop=True)
                        last = nc.tensor.matmul(out[:, 512:640], lhs, t.keys[b:b + HD, v, 5 * P:6 * P], start=True, stop=True)
                    else:
                        last = nc.tensor.matmul(out[:, 0:P], lhs, t.keys[b:b + HD, v, 0:P], start=True, stop=True)
                    last.then_inc(s["tensor"], 1)

                pe.wait_ge(s["scalar"], SCALAR.after("q_staged", i))
                if latent:
                    pe.wait_ge(s["vector"], VECTOR.after("y_copied", i - 1))
                for j in range(PAIRS):
                    last = nc.tensor.transpose(q_bank[:, j * P:(j + 1) * P], q[:, j * P:(j + 1) * P], t.ident[:, :])
                last.then_inc(s["tensor"], 1)
                pe.wait_ge(s["vector"], VECTOR.after("q_copied", i))
                scores(0)
                scores(1)
                for h in range(HEADS):
                    pe.wait_ge(s["scalar"], SCALAR.after(f"exp{h}", i))
                    if h:
                        pe.wait_ge(s["scalar"], SCALAR.after(f"copied{h - 1}", i))
                    for j in range(keys_blocks):
                        out = turned_last[:, 0:P] if j == 4 else turned_bank[:, j * P:(j + 1) * P]
                        last = nc.tensor.transpose(out, probs[h % 2][:, j * P:(j + 1) * P], t.ident[:, :])
                    last.then_inc(s["tensor"], 1)
                    if h + 2 < HEADS:
                        scores(h + 2)
                    pe.wait_ge(s["vector"], VECTOR.after(f"copied{h}", i))
                    pe.wait_ge(s["scalar"], SCALAR.after(f"copied{h}", i))
                    at = (h // 4) * HD
                    for j in range(keys_blocks):
                        v = t.cached_v[:, at:at + HD] if j == 4 else t.qkv[:, j + latent, 640 + at:640 + at + HD]
                        last = nc.tensor.matmul(mixed_bank[:, h * HD:(h + 1) * HD], probs_turned[h % 2][:, j * P:(j + 1) * P], v,
                                                start=(j == 0), stop=(j == keys_blocks - 1))
                    last.then_inc(s["tensor"], 1)
                pe.wait_ge(s["vector"], VECTOR.after("y", i))
                for j in range(PAIRS):
                    last = nc.tensor.transpose(q_bank[:, j * P:(j + 1) * P], y[:, j * P:(j + 1) * P], t.ident[:, :])
                last.then_inc(s["tensor"], 1)

            each_tile(pe, tile)

        @block.vector
        def _(dve):
            def tile(i, latent):
                def bound(h):
                    dve.wait_ge(s["tensor"], TENSOR.after(f"scores{h}", i))
                    nc.vector.tensor_reduce(largest[:, h:h + 1], scores_of[h % 2][:, 0:NK if latent else P], AX, ALU.max).then_inc(s["vector"], 1)
                    dve.wait_ge(s["vector"], VECTOR.after(f"max{h}", i))
                    nc.vector.tensor_scalar(bias[:, h:h + 1], largest[:, h:h + 1], -scale, None, ALU.mult).then_inc(s["vector"], 1)

                dve.wait_ge(s["tensor"], TENSOR.after("q_turned", i))
                nc.vector.tensor_copy(q_turned[:, :, :], q_bank[:, :].rearrange("p (j n) -> p j n", j=PAIRS)).then_inc(s["vector"], 1)
                bound(0)
                bound(1)
                n = 4 * P if latent else P
                for h in range(HEADS):
                    dve.wait_ge(s["tensor"], TENSOR.after(f"turned{h}", i))
                    nc.vector.tensor_copy(probs_turned[h % 2][:, 0:n], turned_bank[:, 0:n]).then_inc(s["vector"], 1)
                    if h + 2 < HEADS:
                        bound(h + 2)
                dve.wait_ge(s["scalar"], SCALAR.after(f"exp{HEADS - 1}", i))
                nc.vector.reciprocal(inverse[:, :], total[:, :]).then_inc(s["vector"], 1)
                dve.wait_ge(s["vector"], VECTOR.after("inverse", i))
                dve.wait_ge(s["tensor"], TENSOR.after(f"mixed{HEADS - 1}", i))
                nc.vector.tensor_tensor(y[:, :].rearrange("p (h e) -> p h e", e=HD), mixed_bank[:, :].rearrange("p (h e) -> p h e", e=HD),
                                        inverse[:, :].unsqueeze(2).to_broadcast([P, HEADS, HD]), ALU.mult).then_inc(s["vector"], 1)
                dve.wait_ge(s["tensor"], TENSOR.after("y_turned", i))
                nc.vector.tensor_copy(t.y_attn[:, :, ds(i * P, P)], q_bank[:, :].rearrange("p (j n) -> p j n", j=PAIRS)).then_inc(s["vector"], 1)

            each_tile(dve, tile)
            dve.wait_ge(s["vector"], VECTOR.all(TILES))

        @block.scalar
        def _(act):
            def tile(i, latent):
                def exponentials(h):
                    act.wait_ge(s["vector"], VECTOR.after(f"bias{h}", i))
                    n = NK if latent else P
                    nc.scalar.activation(probs[h % 2][:, 0:n], scores_of[h % 2][:, 0:n], ACT.Exp, bias=bias[:, h:h + 1],
                                         scale=scale, accum_out=total[:, h:h + 1]).then_inc(s["scalar"], 1)

                if latent:
                    act.wait_ge(s["vector"], VECTOR.after("y", i - 1))
                nc.scalar.copy(q[:, :].unsqueeze(1), t.qkv[:, ds(i, 1), 0:W]).then_inc(s["scalar"], 1)
                exponentials(0)
                for h in range(HEADS):
                    if h + 1 < HEADS:
                        exponentials(h + 1)
                    act.wait_ge(s["tensor"], TENSOR.after(f"turned{h}", i))
                    if latent:
                        nc.scalar.copy(probs_turned[h % 2][:, 4 * P:NK], turned_last[:, 0:P]).then_inc(s["scalar"], 1)
                    else:
                        nc.scalar.copy(unused[:, :], bias[:, h:h + 1]).then_inc(s["scalar"], 1)
                        act.wait_ge(s["scalar"], SCALAR.after(f"copied{h}", i))

            each_tile(act, tile)


ATTENTION = ("tensor", "vector", "scalar")


RW_R, RW_K, RW_V, RW_KK, RW_BONUS, RW_GATE, RW_DIRECTION = 0, 1, 2, 3, 4, 5, 6
RW_BLOCKS = 12


def rwkv_inputs_stage(nc, t, s, before, layer):
    VECTOR = Marks("less_cur", "shifted", "shift_sum", "z", "kk", "kk_sum", "kk_eps", "kk_inverse", "kk_done", "rk", "rk_row", "rk_sum", "bonus",
                   *[f"{n}{d}" for d in range(2) for n in ("w", "a", "removal", "factor", "key")])
    SCALAR = Marks("lora", "kk_square", "gate", "kk_root", "decay_sigmoid0", "decay0", "a0", "decay_sigmoid1", "decay1", "a1")
    W0, A0, K_K, K_A, R_K = 0, 2, 4, 5, 6
    with ExitStack() as mem:
        def sbuf(name, *shape):
            return mem.enter_context(nc.sbuf_tensor("rw_in_" + name, [P, *shape], F32))

        rows, mu, mu_lora = sbuf("rows", 7, W), sbuf("mu", 2, 3 * W), sbuf("mu_lora", 2, 3)
        w2, a2, g2 = sbuf("w2", W), sbuf("a2", W), sbuf("g2", W)
        lora, step = sbuf("lora", 3, NTOK), sbuf("lora_step", 3, LAT)
        cur, prev, following = sbuf("cur", 3 * W), sbuf("prev", 3 * W), sbuf("next", 3 * W)
        z = sbuf("z", 4, W)
        extra = sbuf("extra", 2, W)
        per = [sbuf(f"direction{d}", 3, W) for d in range(2)]
        square, a = sbuf("square", W), sbuf("a", 2, W)
        total, root, inverse, dot = (sbuf(n, HEADS) for n in ("total", "root", "inverse", "dot"))
        lora_tile = sbuf("lora_tile", 3, P)
        block = mem.enter_context(nc.Block())
        stores = (s["z_stored"], s["extra_stored"], s["per0_stored"], s["per1_stored"])

        @block.sync
        def _(sp):
            sp.dma_start(mu_lora[:, :, :], t.dram["mu_lora"][layer, :, :, :]).then_inc(s["mu_loaded"], 16)
            sp.dma_start(rows[:, :, :], t.dram["rw_rows"][layer, 0:7, :].partition_broadcast(P)).then_inc(s["loaded"], 16)
            sp.dma_start(mu[:, :, :], t.dram["mu_rows"][layer, :, :].partition_broadcast(P)).then_inc(s["loaded"], 16)
            for tensor, source in ((w2, t.dram["rw_w2"]), (a2, t.dram["rw_a2"]), (g2, t.dram["rw_g2"])):
                sp.dma_start(tensor[:, :], source[layer, :, :]).then_inc(s["loaded"], 16)

            def load(i):
                for k, buffer in enumerate((prev, cur, following)):
                    sp.dma_start(buffer[:, :], t.dram["rkv_scratch"][ds(i * CORE_ROWS + k, P), :]).then_inc(s["tile_loaded"], 16)

            def store(i):
                at = ds(i * P, P)
                sp.wait_ge(s["vector"], VECTOR.after("kk_done", i))
                sp.sem_inc(s["loads_allowed"], 1)
                sp.dma_start(t.dram["rw_scratch"][at, 0:4, :], z[:, :, :]).then_inc(stores[0], 16)
                sp.wait_ge(s["vector"], VECTOR.after("bonus", i))
                sp.sem_inc(s["loads_allowed"], 1)
                sp.wait_ge(s["scalar"], SCALAR.after("gate", i))
                sp.sem_inc(s["loads_allowed"], 1)
                sp.dma_start(t.dram["rw_scratch"][at, 4:6, :], extra[:, :, :]).then_inc(stores[1], 16)
                for d in range(2):
                    sp.wait_ge(s["vector"], VECTOR.after(f"key{d}", i))
                    sp.sem_inc(s["loads_allowed"], 1)
                    sp.wait_ge(s["scalar"], SCALAR.after(f"decay{d}", i))
                    sp.sem_inc(s["loads_allowed"], 1)
                    sp.dma_start(t.dram["rw_scratch"][at, 6 + 3 * d:9 + 3 * d, :], per[d][:, :, :]).then_inc(stores[2 + d], 16)

            load(0)
            with sp.Fori(1, TILES) as i:
                sp.wait_ge(s["vector"], VECTOR.after("z", i - 1))
                sp.sem_inc(s["loads_allowed"], 1)
                load(i)
                store(i - 1)
            store(TILES - 1)
            for semaphore in stores:
                sp.wait_ge(semaphore, 16 * TILES)

        @block.gpsimd
        def _(pool):
            clear(pool, before)
            pool.wait_ge(s["loaded"], 80)

            def tile(i, repeated):
                pool.wait_ge(s["tile_loaded"], 48 * (i + 1))
                nc.gpsimd.tensor_tensor(following[:, :], following[:, :], cur[:, :], ALU.subtract).then_inc(s["pool"], 1)
                pool.wait_ge(s["pool"], 2 * i + 1)
                nc.gpsimd.tensor_tensor(following[:, :], following[:, :], mu[:, 1, :], ALU.mult).then_inc(s["pool"], 1)

            each_tile(pool, tile)

        @block.tensor
        def _(pe):
            pe.wait_ge(s["loaded"], 80)

            def tile(i, repeated):
                pe.wait_ge(s["scalar"], SCALAR.after("lora", i))
                if repeated:
                    pe.wait_ge(s["vector"], VECTOR.after("a1", i - 1))
                for d in range(2):
                    b = d * HD
                    nc.tensor.matmul(t.bank[d][:, :], lora_tile[b:b + HD, 0, :], w2[b:b + HD, :], start=True, stop=True)
                for d in range(2):
                    b = d * HD
                    nc.tensor.matmul(t.bank[2 + d][:, :], lora_tile[b:b + HD, 1, :], a2[b:b + HD, :], start=True, stop=True)
                nc.tensor.matmul(t.bank[4][:, :], lora_tile[:, 2, :], g2[:, :], start=True, stop=True).then_inc(s["products"], 1)

            each_tile(pe, tile)

        @block.scalar
        def _(act):
            act.wait_ge(s["lora_shifted"], 16)
            nc.scalar.activation(lora[:, 0, :], lora[:, 0, :], ACT.Tanh).then_inc(s["lora_ready"], 1)
            nc.scalar.activation(lora[:, 2, :], lora[:, 2, :], ACT.Sigmoid).then_inc(s["lora_ready"], 1)
            act.wait_ge(s["lora_ready"], 2)

            def tile(i, repeated):
                if repeated:
                    act.wait_ge(s["products"], i)
                nc.scalar.copy(lora_tile[:, :, :], lora[:, :, ds(i * P, P)]).then_inc(s["scalar"], 1)
                act.wait_ge(s["vector"], VECTOR.after("kk", i))
                nc.scalar.activation(square[:, :], z[:, 3, :], ACT.Square).then_inc(s["scalar"], 1)
                act.wait_ge(s["products"], i + 1)
                if repeated:
                    act.wait_ge(stores[1], 16 * i)
                nc.scalar.copy(extra[:, 1, :], t.bank[4][:, :]).then_inc(s["scalar"], 1)
                act.wait_ge(s["vector"], VECTOR.after("kk_eps", i))
                nc.scalar.activation(root[:, :], total[:, :], ACT.Sqrt).then_inc(s["scalar"], 1)
                for d in range(2):
                    act.wait_ge(s["vector"], VECTOR.after(f"w{d}", i))
                    nc.scalar.activation(per[d][:, 0, :], per[d][:, 0, :], ACT.Sigmoid).then_inc(s["scalar"], 1)
                    act.wait_ge(s["scalar"], SCALAR.after(f"decay_sigmoid{d}", i))
                    nc.scalar.mul(per[d][:, 0, :], per[d][:, 0, :], DECAY_SCALE).then_inc(s["scalar"], 1)
                    act.wait_ge(s["vector"], VECTOR.after(f"a{d}", i))
                    nc.scalar.activation(a[:, d, :], a[:, d, :], ACT.Sigmoid).then_inc(s["scalar"], 1)

            each_tile(act, tile)

        @block.vector
        def _(dve):
            dve.wait_ge(s["mu_loaded"], 16)
            done = Steps(dve, s["lora_shifted"])
            for g, (lo, m) in enumerate(GROUPS):
                at = LORA_PAD[g]
                here = t.lora[:, :, at:at + m]
                for k, near in enumerate((t.lora[:, :, at - 1:at - 1 + m], t.lora[:, :, at + 1:at + 1 + m])):
                    done.step(nc.vector.tensor_tensor(step[:, :, 0:m], near, here, ALU.subtract))
                    for j in range(3):
                        done.step(nc.vector.scalar_tensor_tensor(out=lora[:, j, lo:lo + m], in0=step[:, j, 0:m], scalar=mu_lora[:, k, j:j + 1],
                                                                 in1=here[:, j, :] if k == 0 else lora[:, j, lo:lo + m], op0=ALU.mult, op1=ALU.add))
            dve.wait_ge(s["loaded"], 80)

            def heads(ap):
                return ap.rearrange("p (h e) -> p h e", e=HD)

            def spread(ap):
                return ap.unsqueeze(2).to_broadcast([P, HEADS, HD])

            def tile(i, repeated):
                done = Steps(dve, s["vector"], i * len(VECTOR.names))
                v = nc.vector
                dve.wait_ge(s["tile_loaded"], 48 * (i + 1))
                done.step(v.tensor_tensor(prev[:, :], prev[:, :], cur[:, :], ALU.subtract))
                done.step(v.tensor_tensor(prev[:, :], prev[:, :], mu[:, 0, :], ALU.mult))
                done.step(v.tensor_tensor(prev[:, :], prev[:, :], cur[:, :], ALU.add))
                dve.wait_ge(s["pool"], 2 * i + 2)
                if repeated:
                    dve.wait_ge(stores[0], 16 * i)
                done.step(v.tensor_tensor(z[:, 0:3, :], prev[:, :].rearrange("p (j n) -> p j n", j=3),
                                          following[:, :].rearrange("p (j n) -> p j n", j=3), ALU.add))
                r, k, val, kk = (z[:, j, :] for j in range(4))
                done.step(v.tensor_tensor(kk, k, rows[:, K_K, :], ALU.mult))
                dve.wait_ge(s["scalar"], SCALAR.after("kk_square", i))
                done.step(v.tensor_reduce(total[:, :], heads(square[:, :]), AX, ALU.add))
                done.step(v.tensor_scalar(total[:, :], total[:, :], KK_EPS, None, ALU.add))
                dve.wait_ge(s["scalar"], SCALAR.after("kk_root", i))
                done.step(v.reciprocal(inverse[:, :], root[:, :]))
                done.step(v.tensor_tensor(heads(kk), heads(kk), spread(inverse[:, :]), ALU.mult))
                done.step(v.tensor_tensor(square[:, :], r, k, ALU.mult))
                done.step(v.tensor_tensor(square[:, :], square[:, :], rows[:, R_K, :], ALU.mult))
                done.step(v.tensor_reduce(dot[:, :], heads(square[:, :]), AX, ALU.add))
                if repeated:
                    dve.wait_ge(stores[1], 16 * i)
                done.step(v.tensor_tensor(heads(extra[:, 0, :]), heads(val), spread(dot[:, :]), ALU.mult))
                dve.wait_ge(s["products"], i + 1)
                for d in range(2):
                    if repeated:
                        dve.wait_ge(stores[2 + d], 16 * i)
                    done.step(v.tensor_tensor(per[d][:, 0, :], t.bank[d][:, :], rows[:, W0 + d, :], ALU.add))
                    done.step(v.tensor_tensor(a[:, d, :], t.bank[2 + d][:, :], rows[:, A0 + d, :], ALU.add))
                    dve.wait_ge(s["scalar"], SCALAR.after(f"a{d}", i))
                    done.step(v.scalar_tensor_tensor(out=per[d][:, 1, :], in0=kk, scalar=-1.0, in1=a[:, d, :], op0=ALU.mult, op1=ALU.mult))
                    done.step(v.scalar_tensor_tensor(out=a[:, d, :], in0=a[:, d, :], scalar=-1.0, in1=rows[:, K_A, :], op0=ALU.add, op1=ALU.mult))
                    done.step(v.scalar_tensor_tensor(out=per[d][:, 2, :], in0=a[:, d, :], scalar=1.0, in1=k, op0=ALU.add, op1=ALU.mult))
                assert done.n == len(VECTOR.names)

            each_tile(dve, tile)


RWKV_INPUTS = ("mu_loaded", "loaded", "tile_loaded", "vector", "scalar", "products", "pool", "lora_shifted", "lora_ready", "loads_allowed",
               "z_stored", "extra_stored", "per0_stored", "per1_stored")


def wkv_stage(nc, t, s, before, layer):
    QUADS = 2
    LEVELS = 7
    levels = range(1, LEVELS)
    quad_tensor = ["gram_first", "gram_second", "rhs"] + [f"{n}{b}" for b in levels for n in ("inner", "outer")] + ["u", "out"]
    TENSOR = Marks("sums", *[f"turn{p}" for p in range(PAIRS)], *[f"{n}/{q}" for q in range(QUADS) for n in quad_tensor])
    SCALAR = Marks("exps", *[f"turn{p}" for p in range(PAIRS)],
                   *[f"{n}/{q}" for q in range(QUADS) for n in ["rhs"] + [f"inner{b}" for b in levels] + ["u", "out"]])
    VECTOR = Marks("before", "scaled", "state",
                   *[f"{n}/{q}" for q in range(QUADS) for n in ["gram_first", "gram_second", "start"] + [f"outer{b}" for b in levels] + ["end"]])
    POOL = Marks(*[f"level{b}/{q}" for q in range(QUADS) for b in levels])
    with ExitStack() as mem:
        def sbuf(name, *shape):
            return mem.enter_context(nc.sbuf_tensor("wkv_" + name, [P, *shape], F32))

        def both(name, *shape):
            return [sbuf(f"{name}{d}", *shape) for d in range(2)]

        masks = [sbuf(f"masks{d}", 10, P) for d in range(2)]
        halves = sbuf("halves", 4)
        common, own = both("common", 3, W), both("own", 3, W)
        factors = both("factors", 4, W)
        turned = both("turned", PAIRS, 4, P)
        scale = both("scale", PAIRS, 2)
        state = both("state", PAIRS, HD)
        start = both("start", PAIRS, P)
        gram = both("gram", 4, 4, P)
        level = both("level", 3, 4, P)
        inv, inv_turned, inner = both("inv", 4, P), both("inv_turned", 4, P), both("inner", 4, P)
        rhs, u = both("rhs", 4, HD), both("u", 4, HD)
        out = both("out", W)
        block = mem.enter_context(nc.Block())
        loaded, out_stored = (s["loaded0"], s["loaded1"]), (s["out_stored0"], s["out_stored1"])
        tensor_did, scalar_did, vector_did, pool_did = ((s["tensor0"], s["tensor1"]), (s["scalar0"], s["scalar1"]), (s["vector0"], s["vector1"]), (s["pool0"], s["pool1"]))
        state_set = (s["state_set0"], s["state_set1"])
        LOADS = 3

        def each_step(engine, step):
            step(0, (0, 0), False)
            with engine.Fori(1, TILES) as i:
                step(i, (i, TILES - i), True)

        def banks(d):
            return t.bank[4 * d:4 * d + 4]

        def after(engine, semaphores, marks, d, name, i):
            engine.wait_ge(semaphores[d], marks.after(name, i))

        @block.sync
        def _(sp):
            for d in range(2):
                sp.dma_start(masks[d][:, :, :], t.dram["square_constants"][2 + 10 * d:12 + 10 * d, :, :].rearrange("m p n -> p m n")).then_inc(s["constants"], 16)
            sp.dma_start(halves[:, :], t.dram["halves"]).then_inc(s["constants"], 16)

            def load(d, i, at):
                tile = ds(at * P, P)
                sp.dma_start(common[d][:, 0, :], t.dram["rw_scratch"][tile, RW_R, :]).then_inc(loaded[d], 16)
                sp.dma_start(common[d][:, 1:3, :], t.dram["rw_scratch"][tile, RW_V:RW_KK + 1, :]).then_inc(loaded[d], 16)
                sp.dma_start(own[d][:, :, :], t.dram["rw_scratch"][tile, RW_DIRECTION + 3 * d:RW_DIRECTION + 3 * d + 3, :]).then_inc(loaded[d], 16)

            def step(i, tiles, latent):
                tiles = [sp.snap(at) for at in tiles] if latent else tiles
                for d in range(2):
                    if latent:
                        after(sp, tensor_did, TENSOR, d, f"out/{QUADS - 1}", i - 1)
                        after(sp, vector_did, VECTOR, d, "scaled", i - 1)
                        sp.sem_inc(s["loads_allowed"], 1)
                    load(d, i, tiles[d])

            each_step(sp, step)

        @block.gpsimd
        def _(pool):
            clear(pool, before)
            pool.wait_ge(s["constants"], 48)

            def step(i, tiles, latent):
                for q in range(QUADS):
                    for b in levels:
                        for d in range(2):
                            after(pool, vector_did, VECTOR, d, f"gram_second/{q}", i)
                            if b > 3:
                                after(pool, tensor_did, TENSOR, d, f"inner{b - 3}/{q}", i)
                            elif q:
                                after(pool, tensor_did, TENSOR, d, f"inner{b + 3}/{q - 1}", i)
                            elif latent:
                                after(pool, tensor_did, TENSOR, d, f"inner{b + 3}/{QUADS - 1}", i - 1)
                            nc.gpsimd.tensor_tensor(level[d][:, (b - 1) % 3, :, :], gram[d][:, :, 0, :],
                                                    masks[d][:, 3 + b, :].unsqueeze(1).to_broadcast([P, 4, P]), ALU.mult).then_inc(pool_did[d], 1)

            each_step(pool, step)

        @block.tensor
        def _(pe):
            mm = nc.tensor.matmul
            pe.wait_ge(s["constants"], 48)

            def step(i, tiles, latent):
                for d in range(2):
                    pe.wait_ge(loaded[d], 16 * LOADS * (i + 1))
                    if latent:
                        after(pe, scalar_did, SCALAR, d, f"out/{QUADS - 1}", i - 1)
                    A, B, _, _ = banks(d)
                    mm(A, masks[d][:, 0, :], own[d][:, 0, :], start=True, stop=True)
                    for p in range(PAIRS):
                        last = mm(B[:, 2 * p:2 * p + 2], own[d][:, 0, p * P:(p + 1) * P], halves[:, d:d + 2], start=True, stop=True)
                    last.then_inc(tensor_did[d], 1)
                for p in range(PAIRS):
                    for d in range(2):
                        bank = banks(d)[2 + p % 2]
                        if p == 0:
                            after(pe, vector_did, VECTOR, d, "scaled", i)
                            if latent:
                                after(pe, vector_did, VECTOR, d, f"end/{QUADS - 1}", i - 1)
                        if p >= 2:
                            after(pe, scalar_did, SCALAR, d, f"turn{p - 2}", i)
                        for j in range(4):
                            last = nc.tensor.transpose(bank[:, j * P:(j + 1) * P], factors[d][:, j, p * P:(p + 1) * P], t.ident[:, :])
                        last.then_inc(tensor_did[d], 1)
                for q in range(QUADS):
                    for half, name in enumerate(("gram_first", "gram_second")):
                        for d in range(2):
                            if half:
                                after(pe, vector_did, VECTOR, d, f"gram_first/{q}", i)
                            elif q:
                                after(pe, scalar_did, SCALAR, d, f"out/{q - 1}", i)
                                after(pe, vector_did, VECTOR, d, f"end/{q - 1}", i)
                            else:
                                after(pe, scalar_did, SCALAR, d, f"turn{PAIRS - 1}", i)
                            for b in range(2):
                                rows, p = slice(b * HD, b * HD + HD), 2 * q + half
                                alpha_rho = turned[d][rows, p, 0:2, :].rearrange("p a n -> p (a n)")
                                main, side = banks(d)[b], banks(d)[2 + b]
                                mm(main[:, 0:2 * P], turned[d][rows, p, 2, :], alpha_rho, start=True, stop=True)
                                mm(main[:, 2 * P:4 * P], turned[d][rows, p, 3, :], alpha_rho, start=True, stop=True)
                                last = mm(side[:, half * P:(half + 1) * P], turned[d][rows, p, 0, :], turned[d][rows, p, 2, :], start=True, stop=True)
                            last.then_inc(tensor_did[d], 1)
                    for d in range(2):
                        after(pe, vector_did, VECTOR, d, f"start/{q}", i)
                        D = banks(d)[3]
                        for half in range(2):
                            p = 2 * q + half
                            for b in range(2):
                                h = 2 * half + b
                                mm(D[:, h * HD:(h + 1) * HD], turned[d][:, p, 0, :], start[d][:, p, b * HD:(b + 1) * HD], start=True, stop=False)
                                last = mm(D[:, h * HD:(h + 1) * HD], gram[d][:, h, 2, :], common[d][:, 1, (4 * q + h) * HD:(4 * q + h + 1) * HD],
                                          start=False, stop=True)
                        last.then_inc(tensor_did[d], 1)
                    for b in levels:
                        for d in range(2):
                            after(pe, pool_did, POOL, d, f"level{b}/{q}", i)
                            if b > 1:
                                after(pe, vector_did, VECTOR, d, f"outer{b - 1}/{q}", i)
                            for h in range(4):
                                last = mm(banks(d)[0][:, h * P:(h + 1) * P], level[d][:, (b - 1) % 3, h, :], inv[d][:, h, :], start=True, stop=True)
                            last.then_inc(tensor_did[d], 1)
                        for d in range(2):
                            after(pe, scalar_did, SCALAR, d, f"inner{b}/{q}", i)
                            for h in range(4):
                                if b < LEVELS - 1:
                                    mm(banks(d)[1][:, h * P:(h + 1) * P], inv_turned[d][:, h, :], inner[d][:, h, :], start=True, stop=True)
                                last = mm(banks(d)[2][:, h * P:(h + 1) * P], inner[d][:, h, :], inv_turned[d][:, h, :], start=True, stop=True)
                            last.then_inc(tensor_did[d], 1)
                    for d in range(2):
                        after(pe, vector_did, VECTOR, d, f"outer{LEVELS - 1}/{q}", i)
                        for h in range(4):
                            last = mm(banks(d)[0][:, h * HD:(h + 1) * HD], inv_turned[d][:, h, :], rhs[d][:, h, :], start=True, stop=True)
                        last.then_inc(tensor_did[d], 1)
                    for d in range(2):
                        after(pe, scalar_did, SCALAR, d, f"u/{q}", i)
                        _, B, C, _ = banks(d)
                        for half in range(2):
                            p = 2 * q + half
                            for b in range(2):
                                h = 2 * half + b
                                cols = slice(h * HD, (h + 1) * HD)
                                mm(B[:, cols], turned[d][:, p, 1, :], start[d][:, p, b * HD:(b + 1) * HD], start=True, stop=False)
                                mm(B[:, cols], gram[d][:, h, 3, :], common[d][:, 1, (4 * q + h) * HD:(4 * q + h + 1) * HD],
                                   start=False, stop=False)
                                mm(B[:, cols], gram[d][:, h, 1, :], u[d][:, h, :], start=False, stop=True)
                        for half in range(2):
                            p = 2 * q + half
                            mm(C[:, half * P:(half + 1) * P], factors[d][:, 3, p * P:(p + 1) * P], common[d][:, 1, p * P:(p + 1) * P],
                               start=True, stop=False)
                            last = mm(C[:, half * P:(half + 1) * P], factors[d][:, 2, p * P:(p + 1) * P],
                                      u[d][:, 2 * half:2 * half + 2, :].rearrange("p h e -> p (h e)"), start=False, stop=True)
                        last.then_inc(tensor_did[d], 1)

            each_step(pe, step)

        @block.scalar
        def _(act):
            def step(i, tiles, latent):
                for d in range(2):
                    after(act, vector_did, VECTOR, d, "before", i)
                    A, B, _, _ = banks(d)
                    nc.scalar.activation(factors[d][:, 0, :], factors[d][:, 0, :], ACT.Exp)
                    nc.scalar.activation(factors[d][:, 1, :], A, ACT.Exp)
                    nc.scalar.activation(factors[d][:, 2, :], A, ACT.Exp, scale=-1.0)
                    nc.scalar.activation(scale[d][:, :, :], B[:, 0:2 * PAIRS].rearrange("p (j n) -> p j n", n=2), ACT.Exp).then_inc(scalar_did[d], 1)
                for p in range(PAIRS):
                    for d in range(2):
                        after(act, tensor_did, TENSOR, d, f"turn{p}", i)
                        nc.scalar.copy(turned[d][:, p, :, :], banks(d)[2 + p % 2].rearrange("p (j n) -> p j n", j=4)).then_inc(scalar_did[d], 1)
                for q in range(QUADS):
                    for d in range(2):
                        after(act, tensor_did, TENSOR, d, f"rhs/{q}", i)
                        nc.scalar.copy(rhs[d][:, :, :], banks(d)[3][:, 0:4 * HD].rearrange("p (h e) -> p h e", e=HD)).then_inc(scalar_did[d], 1)
                    for b in levels:
                        for d in range(2):
                            after(act, tensor_did, TENSOR, d, f"inner{b}/{q}", i)
                            nc.scalar.copy(inner[d][:, :, :], banks(d)[0].rearrange("p (h n) -> p h n", h=4)).then_inc(scalar_did[d], 1)
                    for d in range(2):
                        after(act, tensor_did, TENSOR, d, f"u/{q}", i)
                        nc.scalar.copy(u[d][:, :, :], banks(d)[0][:, 0:4 * HD].rearrange("p (h e) -> p h e", e=HD)).then_inc(scalar_did[d], 1)
                    for d in range(2):
                        after(act, tensor_did, TENSOR, d, f"out/{q}", i)
                        if latent and q == 0:
                            act.wait_ge(out_stored[d], 16 * i)
                        nc.scalar.copy(out[d][:, q * 4 * HD:(q + 1) * 4 * HD], banks(d)[1][:, 0:4 * HD]).then_inc(scalar_did[d], 1)
                for d in range(2):
                    after(act, scalar_did, SCALAR, d, f"out/{QUADS - 1}", i)
                    act.dma_start(t.dram["out_scratch"][d, ds(tiles[d] * P, P), :], out[d][:, :]).then_inc(out_stored[d], 16)
                    if not latent:
                        after(act, vector_did, VECTOR, d, f"end/{QUADS - 1}", i)
                        act.dma_start(t.dram["state_out"][layer, d, :, :, :].rearrange("j p e -> p j e"), state[d][:, :, :]).then_inc(s["state_stored"], 16)
                if not latent:
                    act.wait_ge(s["state_stored"], 32)
                    for d in range(2):
                        act.dma_start(state[d][:, :, :], t.dram["state_in"][layer, d, :, :, :].rearrange("j p e -> p j e")).then_inc(state_set[d], 16)

            each_step(act, step)
            for d in range(2):
                act.wait_ge(out_stored[d], 16 * TILES)

        @block.vector
        def _(dve):
            v = nc.vector
            for d in range(2):
                v.memset(start[d][:, :, :], 0.0).then_inc(s["zeroed"], 1)
                v.memset(state[d][:, :, :], 0.0).then_inc(s["zeroed"], 1)
            dve.wait_ge(s["zeroed"], 4)
            dve.wait_ge(s["constants"], 48)
            steps = 64

            def step(i, tiles, latent):
                done = Steps(dve, s["vector_steps"], i * steps)
                for d in range(2):
                    after(dve, tensor_did, TENSOR, d, "sums", i)
                    v.tensor_tensor(factors[d][:, 0, :], banks(d)[0], own[d][:, 0, :], ALU.subtract).then_inc(vector_did[d], 1)
                for d in range(2):
                    after(dve, scalar_did, SCALAR, d, "exps", i)
                    done.step(v.tensor_tensor(factors[d][:, 3, :], factors[d][:, 2, :], own[d][:, 2, :], ALU.mult))
                    done.step(v.tensor_tensor(factors[d][:, 2, :], factors[d][:, 2, :], own[d][:, 1, :], ALU.mult))
                    done.step(v.tensor_tensor(factors[d][:, 0, :], factors[d][:, 0, :], common[d][:, 2, :], ALU.mult))
                    v.tensor_tensor(factors[d][:, 1, :], factors[d][:, 1, :], common[d][:, 0, :], ALU.mult).then_inc(vector_did[d], 1)
                    if latent:
                        dve.wait_ge(state_set[d], 16)
                    for b in range(2):
                        rows = slice(b * HD, b * HD + HD)
                        last = v.tensor_tensor(start[d][rows, :, rows], state[d][rows, :, :],
                                               scale[d][rows, :, 0:1].to_broadcast([HD, PAIRS, HD]), ALU.mult)
                        if b == 0:
                            done.step(last)
                    last.then_inc(vector_did[d], 1)
                    after(dve, vector_did, VECTOR, d, "state", i)
                for q in range(QUADS):
                    for half, name in enumerate(("gram_first", "gram_second")):
                        for d in range(2):
                            after(dve, tensor_did, TENSOR, d, f"{name}/{q}", i)
                            keep = masks[d][:, 1:3, :].rearrange("p a n -> p (a n)").unsqueeze(1).to_broadcast([P, 2, 2 * P])
                            for b in range(2):
                                last = v.tensor_tensor(gram[d][:, 2 * half + b, :, :].rearrange("p (c a) n -> p c (a n)", c=2),
                                                       banks(d)[b].rearrange("p (c n) -> p c n", c=2), keep, ALU.mult)
                                if b == 0:
                                    done.step(last)
                            last.then_inc(vector_did[d], 1)
                    for d in range(2):
                        after(dve, vector_did, VECTOR, d, f"gram_second/{q}", i)
                        same = t.ident[:, :].unsqueeze(1).to_broadcast([P, 4, P])
                        for b in range(2):
                            done.step(v.tensor_tensor(inv[d][:, b::2, :], banks(d)[2 + b][:, 0:2 * P].rearrange("p (h n) -> p h n", h=2),
                                                      masks[1 - d][:, 3, :].unsqueeze(1).to_broadcast([P, 2, P]), ALU.mult))
                        done.step(v.tensor_tensor(inv[d][:, :, :], inv[d][:, :, :], same, ALU.add))
                        done.step(v.tensor_tensor(inv_turned[d][:, :, :], gram[d][:, :, 0, :],
                                                  masks[d][:, 3, :].unsqueeze(1).to_broadcast([P, 4, P]), ALU.mult))
                        v.tensor_tensor(inv_turned[d][:, :, :], inv_turned[d][:, :, :], same, ALU.add).then_inc(vector_did[d], 1)
                    for b in levels:
                        for d in range(2):
                            after(dve, tensor_did, TENSOR, d, f"outer{b}/{q}", i)
                            if b == 1:
                                after(dve, vector_did, VECTOR, d, f"start/{q}", i)
                            else:
                                after(dve, vector_did, VECTOR, d, f"outer{b - 1}/{q}", i)
                            if b < LEVELS - 1:
                                done.step(v.tensor_tensor(inv[d][:, :, :], inv[d][:, :, :], banks(d)[1].rearrange("p (h n) -> p h n", h=4), ALU.add))
                            v.tensor_tensor(inv_turned[d][:, :, :], inv_turned[d][:, :, :], banks(d)[2].rearrange("p (h n) -> p h n", h=4),
                                            ALU.add).then_inc(vector_did[d], 1)
                    for d in range(2):
                        after(dve, tensor_did, TENSOR, d, f"out/{q}", i)
                        for b in range(2):
                            rows, pairs = slice(b * HD, b * HD + HD), slice(2 * q, 2 * q + 2)
                            fresh = banks(d)[2][rows, 0:2 * P].rearrange("p (j n) -> p j n", j=2)[:, :, rows]
                            done.step(v.tensor_tensor(state[d][rows, pairs, :], fresh, start[d][rows, pairs, rows], ALU.add))
                            last = v.tensor_tensor(state[d][rows, pairs, :], state[d][rows, pairs, :],
                                                   scale[d][rows, pairs, 1:2].to_broadcast([HD, 2, HD]), ALU.mult)
                            if b == 0:
                                done.step(last)
                        last.then_inc(vector_did[d], 1)
                        after(dve, vector_did, VECTOR, d, f"end/{q}", i)
                assert done.n == steps

            each_step(dve, step)


WKV = ("constants", "loaded0", "loaded1", "out_stored0", "out_stored1", "tensor0", "tensor1", "scalar0", "scalar1", "vector0", "vector1",
       "pool0", "pool1", "state_set0", "state_set1", "state_stored", "zeroed", "loads_allowed", "vector_steps")


def rwkv_output_stage(nc, t, s, before, layer):
    VECTOR = Marks("sum", "head_sum", "mean", "centred", "head_square", "eps", "inverse", "normed", "weighted", "biased", "bonus", "y", "y_copied")
    SCALAR = Marks("square", "root")
    with ExitStack() as mem:
        def sbuf(name, *shape):
            return mem.enter_context(nc.sbuf_tensor("rw_out_" + name, [P, *shape], F32))

        rows = sbuf("rows", 2, W)
        outs, extra, o, square, y = sbuf("outs", 2, W), sbuf("extra", 2, W), sbuf("o", W), sbuf("square", W), sbuf("y", W)
        total, root, inverse = (sbuf(n, HEADS) for n in ("total", "root", "inverse"))
        block = mem.enter_context(nc.Block())

        @block.sync
        def _(sp):
            sp.dma_start(rows[:, :, :], t.dram["rw_rows"][layer, 7:9, :].partition_broadcast(P)).then_inc(s["rows_loaded"], 16)

            def tile(i, repeated):
                if repeated:
                    sp.wait_ge(s["vector"], VECTOR.after("y", i - 1))
                at = ds(i * P, P)
                sp.dma_start(outs[:, :, :], t.dram["out_scratch"][:, at, :].rearrange("d p n -> p d n")).then_inc(s["loaded"], 16)
                sp.dma_start(extra[:, :, :], t.dram["rw_scratch"][at, RW_BONUS:RW_GATE + 1, :]).then_inc(s["loaded"], 16)

            each_tile(sp, tile)

        @block.gpsimd
        def _(pool):
            clear(pool, before)

        @block.tensor
        def _(pe):
            def tile(i, repeated):
                pe.wait_ge(s["vector"], VECTOR.after("y", i))
                for j in range(4):
                    last = nc.tensor.transpose(t.bank[0][:, j * P:(j + 1) * P], y[:, j * P:(j + 1) * P], t.ident[:, :])
                last.then_inc(s["turned"], 1)

            each_tile(pe, tile)

        @block.scalar
        def _(act):
            def tile(i, repeated):
                act.wait_ge(s["vector"], VECTOR.after("centred", i))
                nc.scalar.activation(square[:, :], o[:, :], ACT.Square).then_inc(s["scalar"], 1)
                act.wait_ge(s["vector"], VECTOR.after("eps", i))
                nc.scalar.activation(root[:, :], total[:, :], ACT.Sqrt).then_inc(s["scalar"], 1)

            each_tile(act, tile)

        @block.vector
        def _(dve):
            v = nc.vector
            dve.wait_ge(s["rows_loaded"], 16)

            def tile(i, repeated):
                done = Steps(dve, s["vector"], i * len(VECTOR.names))
                heads = o[:, :].rearrange("p (h e) -> p h e", e=HD)
                dve.wait_ge(s["loaded"], 32 * (i + 1))
                done.step(v.tensor_tensor(o[:, :], outs[:, 0, :], outs[:, 1, :], ALU.add))
                done.step(v.tensor_reduce(total[:, :], heads, AX, ALU.add))
                done.step(v.tensor_scalar(total[:, :], total[:, :], -1.0 / HD, None, ALU.mult))
                done.step(v.tensor_tensor(heads, heads, total[:, :].unsqueeze(2).to_broadcast([P, HEADS, HD]), ALU.add))
                dve.wait_ge(s["scalar"], SCALAR.after("square", i))
                done.step(v.tensor_reduce(total[:, :], square[:, :].rearrange("p (h e) -> p h e", e=HD), AX, ALU.add))
                done.step(v.tensor_scalar(total[:, :], total[:, :], 1.0 / HD, GN_EPS, ALU.mult, ALU.add))
                dve.wait_ge(s["scalar"], SCALAR.after("root", i))
                done.step(v.reciprocal(inverse[:, :], root[:, :]))
                done.step(v.tensor_tensor(heads, heads, inverse[:, :].unsqueeze(2).to_broadcast([P, HEADS, HD]), ALU.mult))
                done.step(v.tensor_tensor(o[:, :], o[:, :], rows[:, 0, :], ALU.mult))
                done.step(v.tensor_tensor(o[:, :], o[:, :], rows[:, 1, :], ALU.add))
                done.step(v.tensor_tensor(o[:, :], o[:, :], extra[:, 0, :], ALU.add))
                done.step(v.tensor_tensor(y[:, :], o[:, :], extra[:, 1, :], ALU.mult))
                dve.wait_ge(s["turned"], i + 1)
                done.step(v.tensor_copy(t.y_rw[:, :, ds(i * P, P)], t.bank[0].rearrange("p (j n) -> p j n", j=4)))

            each_tile(dve, tile)


RWKV_OUTPUT = ("rows_loaded", "loaded", "turned", "vector", "scalar")


def merge_stage(nc, t, s, before, layer):
    RING = 4
    UNITS = 6
    with ExitStack() as mem:
        def sbuf(name, *shape):
            return mem.enter_context(nc.sbuf_tensor("merge_" + name, [P, *shape], F32))

        gate_weights = [sbuf(f"gate_weights{b}", 3, KD, P) for b in range(2)]
        out_weights = [sbuf(f"out_weights{b}", 3, 4, P) for b in range(2)]
        last_weights = [sbuf(f"last_weights{b}", KD, 512) for b in range(2)]
        merged = sbuf("merged", KD, NTOK)
        sigmoid, product = [sbuf(f"sigmoid{b}", LAT) for b in range(2)], sbuf("product", LAT)
        block = mem.enter_context(nc.Block())
        branches = (t.y_rw, t.y_conv, t.y_attn)
        units = [(g, r) for g in range(2) for r in range(3)]
        loaded = (s["loaded0"], s["loaded1"])

        @block.sync
        def _(sp):
            with sp.Fori(0, KD // 2) as i:
                for b in range(2):
                    sp.wait_ge(s["product"], (i * 2 + b + 1) * UNITS)
                    sp.sem_inc(s["held"], 1)
                    for r in range(3):
                        sp.dma_start(gate_weights[b][:, r, :, :],
                                     t.dram["w_in"][layer, :, :].rearrange("(k p) n -> p k n", p=P)[:, :, ds((i * 2 + b) * P + COL_GATE + r * D, P)]
                                     ).then_inc(loaded[b], 16)
                        sp.dma_start(out_weights[b][:, r, :, :],
                                     t.dram["w_out"][layer, r, :, :].rearrange("(k p) n -> p k n", p=P)[:, :, ds((i * 2 + b) * P, P)]
                                     ).then_inc(loaded[b], 16)
            for c in range(2):
                sp.dma_start(last_weights[c][:, :, :], t.dram["w_o"][layer, :, c * 512:(c + 1) * 512].rearrange("(k p) n -> p k n", p=P)
                             ).then_inc(s["last_loaded"], 16)

        @block.gpsimd
        def _(pool):
            clear(pool, before)

        @block.tensor
        def _(pe):
            pe.sem_inc(s["product"], 2 * UNITS)
            with pe.Fori(0, KD // 2) as i:
                for b in range(2):
                    pe.wait_ge(loaded[b], (i + 1) * 96)
                    for n, (g, r) in enumerate(units):
                        lo, m = GROUPS[g]
                        slot = (b * UNITS + n) % RING
                        pe.wait_ge(s["gated"], (i * 2 + b) * UNITS + n + 1)
                        for k in range(KD):
                            nc.tensor.matmul(t.bank[2 * slot][:, 0:m], gate_weights[b][:, r, k, :], t.h[:, k, lo:lo + m],
                                             start=(k == 0), stop=(k == KD - 1))
                        for k in range(4):
                            last = nc.tensor.matmul(t.bank[2 * slot + 1][:, 0:m], out_weights[b][:, r, k, :], branches[r][:, k, lo:lo + m],
                                                    start=(k == 0), stop=(k == 3))
                        last.then_inc(s["product"], 1)
            pe.wait_ge(s["added"], KD * 4)
            pe.wait_ge(s["last_loaded"], 32)
            for n in range(2 * TILES):
                c, i = n // TILES, n % TILES
                if n >= 8:
                    pe.wait_ge(s["residual"], 2 * (n - 8) + 1)
                for k in range(KD):
                    last = nc.tensor.matmul(t.bank[n % 8][:, :], merged[:, k, i * P:(i + 1) * P], last_weights[c][:, k, :],
                                            start=(k == 0), stop=(k == KD - 1))
                last.then_inc(s["projected"], 1)

        @block.scalar
        def _(act):
            with act.Fori(0, KD // 2) as i:
                for b in range(2):
                    for n, (g, r) in enumerate(units):
                        at = b * UNITS + n
                        act.wait_ge(s["product"], i * 2 * UNITS + at + 1 + 2 * UNITS)
                        act.wait_ge(s["gated"], i * 2 * UNITS + at + 3)
                        m = GROUPS[g][1]
                        nc.scalar.activation(sigmoid[at % 2][:, 0:m], t.bank[2 * (at % RING)][:, 0:m], ACT.Sigmoid).then_inc(s["sigmoid"], 1)

        @block.vector
        def _(dve):
            dve.sem_inc(s["gated"], RING)
            with dve.Fori(0, KD // 2) as i:
                for b in range(2):
                    adds = (i * 2 + b) * 4
                    for n, (g, r) in enumerate(units):
                        at = b * UNITS + n
                        lo, m = GROUPS[g]
                        dve.wait_ge(s["sigmoid"], i * 2 * UNITS + at + 1)
                        out = merged[:, ds(i * 2 + b, 1), lo:lo + m]
                        target = out if r == 0 else product[:, 0:m].unsqueeze(1)
                        nc.vector.tensor_tensor(target, sigmoid[at % 2][:, 0:m].unsqueeze(1), t.bank[2 * (at % RING) + 1][:, 0:m].unsqueeze(1),
                                                ALU.mult).then_inc(s["gated"], 1)
                        if r:
                            dve.wait_ge(s["gated"], i * 2 * UNITS + at + 1 + RING)
                            nc.vector.tensor_tensor(out, out, target, ALU.add).then_inc(s["added"], 1)
                            dve.wait_ge(s["added"], adds + g * 2 + r)
            for n in range(2 * TILES):
                c, i = n // TILES, n % TILES
                cols = slice(c * 512, (c + 1) * 512)
                dve.wait_ge(s["projected"], n + 1)
                nc.vector.tensor_tensor(product[:, :], t.bank[n % 8][:, :], t.gate_rows[:, 0, min(i, 1), cols], ALU.mult).then_inc(s["residual"], 1)
                dve.wait_ge(s["residual"], 2 * n + 1)
                nc.vector.tensor_tensor(t.x[:, i, cols], t.x[:, i, cols], product[:, :], ALU.add).then_inc(s["residual"], 1)
                dve.wait_ge(s["residual"], 2 * n + 2)


MERGE = ("held", "loaded0", "loaded1", "last_loaded", "gated", "product", "added", "residual", "projected", "sigmoid")


def peer_query_stage(nc, t, s, before, layer):
    with ExitStack() as mem:
        def sbuf(name, *shape):
            return mem.enter_context(nc.sbuf_tensor("query_" + name, [P, *shape], F32))

        weights = [sbuf(f"weights{b}", KD, 512) for b in range(2)]
        keys, queries = sbuf("keys", HEADS, KEYS), sbuf("queries", HEADS, NTOK)
        rows = [sbuf(f"rows{b}", D) for b in range(2)]
        scores = [sbuf(f"scores{b}", HEADS, 2, KEYS) for b in range(2)]
        block = mem.enter_context(nc.Block())
        stored = (s["rows_stored0"], s["rows_stored1"], s["scores_stored0"], s["scores_stored1"])

        @block.sync
        def _(sp):
            for c in range(2):
                sp.dma_start(weights[c][:, :, :], t.dram["peer_wq"][layer, :, c * 512:(c + 1) * 512].rearrange("(k p) n -> p k n", p=P)
                             ).then_inc(s["loaded"], 16)
            sp.dma_start(keys[:, :, :], t.dram["peer_keys"][layer, :, :, :]).then_inc(s["keys_loaded"], 16)
            for i in range(TILES):
                sp.wait_ge(s["row_copied"], 2 * (i + 1))
                sp.dma_start(t.dram["h_scratch"][i * P:(i + 1) * P, :], rows[i % 2][:, :]).then_inc(stored[i % 2], 16)
            for i in range(TILES):
                sp.wait_ge(s["scores_copied"], 4 * (i + 1))
                repeats = 2 if i == TILES - 1 else 1
                sp.dma_start(t.dram["score_scratch"][i * HEADS:(i + 1) * HEADS, :, :, :].rearrange("h p c n -> p h (c n)"),
                             scores[i % 2][:, :, :, :].rearrange("p h c n -> p h (c n)")).then_inc(stored[2 + i % 2], 16)
                if repeats == 2:
                    sp.dma_start(t.dram["score_scratch"][TILES * HEADS, :, :, :], scores[i % 2][:, HEADS - 1, :, :]).then_inc(stored[2 + i % 2], 16)
            sp.wait_ge(stored[0], 48)
            sp.wait_ge(stored[1], 32)
            sp.wait_ge(stored[2], 64)
            sp.wait_ge(stored[3], 32)

        @block.gpsimd
        def _(pool):
            clear(pool, before)

        @block.tensor
        def _(pe):
            for i in range(TILES):
                if i >= 2:
                    pe.wait_ge(s["row_copied"], 2 * (i - 1))
                for half in range(2):
                    for k in range(4):
                        last = nc.tensor.transpose(t.bank[2 * (i % 2) + half][:, k * P:(k + 1) * P], t.h[:, 4 * half + k, i * P:(i + 1) * P], t.ident[:, :])
                    last.then_inc(s["turned"], 1)
            pe.wait_ge(s["loaded"], 32)
            for n in range(2 * HEADS):
                h, g = n // 2, n % 2
                lo, m = GROUPS[g]
                if n >= 4:
                    pe.wait_ge(s["query_copied"], n - 3)
                for k in range(KD):
                    last = nc.tensor.matmul(t.bank[4 + n % 4][:, 0:m], weights[h // 4][:, k, (h % 4) * P:(h % 4 + 1) * P], t.h[:, k, lo:lo + m],
                                            start=(k == 0), stop=(k == KD - 1))
                last.then_inc(s["query"], 1)
            pe.wait_ge(s["query_copied"], 2 * HEADS)
            pe.wait_ge(s["row_copied"], 2 * TILES)
            pe.wait_ge(s["keys_loaded"], 16)
            for i in range(TILES):
                for c in range(2):
                    for quad in range(2):
                        if i >= 2:
                            pe.wait_ge(s["scores_copied"], 4 * (i - 2) + 2 * c + quad + 1)
                        for h in range(4 * quad, 4 * quad + 4):
                            last = nc.tensor.matmul(t.bank[4 * (i % 2) + 2 * c + quad][:, (h % 4) * P:(h % 4 + 1) * P],
                                                    queries[c * HD:(c + 1) * HD, h, i * P:(i + 1) * P], keys[c * HD:(c + 1) * HD, h, :],
                                                    start=True, stop=True)
                        last.then_inc(s["scored"], 1)

        @block.vector
        def _(dve):
            for i in range(TILES):
                for half in range(2):
                    dve.wait_ge(s["turned"], 2 * i + half + 1)
                    if i >= 2:
                        dve.wait_ge(stored[i % 2], 16 * (i // 2))
                    nc.vector.tensor_copy(rows[i % 2][:, half * 512:(half + 1) * 512], t.bank[2 * (i % 2) + half][:, :]).then_inc(s["row_copied"], 1)
            for i in range(TILES):
                for c in range(2):
                    for quad in range(2):
                        dve.wait_ge(s["scored"], 4 * i + 2 * c + quad + 1)
                        if i >= 2:
                            dve.wait_ge(stored[2 + i % 2], 16 * (i // 2))
                        nc.vector.tensor_copy(scores[i % 2][:, 4 * quad:4 * quad + 4, c, :],
                                              t.bank[4 * (i % 2) + 2 * c + quad].rearrange("p (h n) -> p h n", h=4)).then_inc(s["scores_copied"], 1)

        @block.scalar
        def _(act):
            for n in range(2 * HEADS):
                h, g = n // 2, n % 2
                lo, m = GROUPS[g]
                act.wait_ge(s["query"], n + 1)
                nc.scalar.copy(queries[:, h, lo:lo + m], t.bank[4 + n % 4][:, 0:m]).then_inc(s["query_copied"], 1)


PEER_QUERY = ("loaded", "keys_loaded", "row_copied", "scores_copied", "turned", "query_copied", "query", "scored",
              "rows_stored0", "rows_stored1", "scores_stored0", "scores_stored1")


def peer_stage(nc, t, s, before, layer):
    RING = 8
    DIAGONALS = 8
    LOWEST = -3.0e38
    LOOKUP = 26
    TURNS = TOPK // RING
    with ExitStack() as mem:
        def sbuf(name, *shape, dtype=F32):
            return mem.enter_context(nc.sbuf_tensor("peer_" + name, [P, *shape], dtype))

        def both(name, *shape, dtype=F32):
            return [sbuf(f"{name}{b}", *shape, dtype=dtype) for b in range(2)]

        h = sbuf("h", D)
        scores, rest = both("scores", 2, KEYS), sbuf("rest", 2, KEYS)
        best, best_at = sbuf("best", 2, TOPK), sbuf("best_at", 2, TOPK, dtype=U32)
        sums, sums_rest = sbuf("sums", TOPK, TOPK), sbuf("sums_rest", TOPK * TOPK)
        top, top_at = both("top", TOPK), sbuf("top_at", TOPK, dtype=U32)
        place = sbuf("place", 2, TOPK, dtype=U32)
        chosen, expert = sbuf("chosen", TOPK, TOPK), sbuf("expert", 2, TOPK)
        number = sbuf("number", TOPK)
        index = both("index", TOPK, dtype=U32)
        least, total, inverse = both("least", 1), both("total", 1), both("inverse", 1)
        power, dots, active, weight = both("power", TOPK), both("dots", TOPK), both("active", TOPK), both("weight", TOPK)
        iota = sbuf("iota", TOPK)
        u_rows, v_rows = [sbuf(f"u_rows{k}", D) for k in range(RING)], [sbuf(f"v_rows{k}", D) for k in range(RING)]
        diagonal = [sbuf(f"diagonal{k}", P) for k in range(DIAGONALS)]
        zeros = sbuf("zeros", 512)
        block = mem.enter_context(nc.Block())
        u_landed, v_landed = ([s[f"{n}_landed{k}"] for k in range(RING)] for n in "uv")
        scores_loaded = (s["scores_loaded0"], s["scores_loaded1"])

        def passes(engine, before_tile, one, after_tile):
            with engine.Fori(0, TILES) as i:
                before_tile(i)
                with engine.Fori(0, PAIRS) as j:
                    for b in range(2):
                        one((i * PAIRS + j) * 2 + b, b)
                after_tile(i)

        def nothing(i):
            pass

        @block.sync
        def _(sp):
            def load(n, b):
                sp.dma_start(scores[b][:, :, :], t.dram["score_scratch"][n, :, :, :] if isinstance(n, int) else
                             t.dram["score_scratch"][ds(n, 1), :, :, :].rearrange("a p c n -> p (a c) n")).then_inc(scores_loaded[b], 16)

            sp.dma_start(iota[:, :], t.dram["iota"].partition_broadcast(P)).then_inc(s["iota_loaded"], 16)
            load(0, 0)

            def tile(i):
                sp.wait_ge(s["tile_done"], i + 1)
                sp.sem_inc(s["held"], 1)
                sp.dma_start(h[:, :], t.dram["h_scratch"][ds(i * P, P), :]).then_inc(s["h_loaded"], 16)

            def one(n, b):
                sp.wait_ge(s["looked_up"], n + 1)
                sp.sem_inc(s["held"], 1)
                load(n + 1, 1 - b)

            passes(sp, tile, one, nothing)

        @block.gpsimd
        def _(pool):
            clear(pool, before)

            def one(n, b):
                pool.wait_ge(s["looked_up"], n + 2)
                for table, rows, landed, used in ((t.dram["peer_u"], u_rows, u_landed, s["dotted"]), (t.dram["peer_v"], v_rows, v_landed, s["mixed"])):
                    for k in range(TOPK):
                        if k % (RING // 2) == 0:
                            pool.wait_ge(used, n * TOPK + k + RING // 2)
                            pool.sem_inc(s["held_pool"], 1)
                        nc.gpsimd.indirect_dma_start(rows[k % RING][:, :], None, table,
                                                     bass.IndirectOffsetOnAxis(ap=index[b][:, k:k + 1], axis=0)).then_inc(landed[k % RING], 16)

            passes(pool, nothing, one, nothing)

        @block.tensor
        def _(pe):
            pe.wait_ge(s["zeroed"], 1)
            pe.sem_inc(s["mixed"], RING)

            def open_tile(i):
                pe.wait_ge(s["emptied"], i + 1)
                for c in range(2):
                    nc.tensor.matmul(t.bank[c], zeros[:, 0:P], zeros[:, :], start=True, stop=False)

            def one(n, b):
                for k in range(TOPK):
                    pe.wait_ge(v_landed[k % RING], (n * TURNS + k // RING + 1) * 16)
                    pe.wait_ge(s["diagonal"], n * TOPK + k + 1)
                    for c in range(2):
                        last = nc.tensor.matmul(t.bank[c], diagonal[k % DIAGONALS][:, :], v_rows[k % RING][:, c * 512:(c + 1) * 512], start=False, stop=False)
                    last.then_inc(s["mixed"], 1)

            def close_tile(i):
                for c in range(2):
                    last = nc.tensor.matmul(t.bank[c], zeros[:, 0:P], zeros[:, :], start=False, stop=True)
                last.then_inc(s["tile_mixed"], 1)

            passes(pe, open_tile, one, close_tile)

        @block.scalar
        def _(act):
            def soften(n, b):
                act.wait_ge(s["looked_up"], n + 2)
                nc.scalar.activation(power[b][:, :], top[b][:, :], ACT.Exp, bias=least[b][:, 0:1], accum_out=total[b][:, 0:1]).then_inc(s["powers"], 1)

            soften(0, 0)

            def one(n, b):
                soften(n + 1, 1 - b)
                act.wait_ge(s["dotted"], n * TOPK + TOPK + RING)
                nc.scalar.activation(active[b][:, :], dots[b][:, :], ACT.Gelu).then_inc(s["activated"], 1)
                act.wait_ge(s["weighed"], n + 1)
                for k in range(TOPK):
                    act.wait_ge(s["mixed"], n * TOPK + k + 1)
                    nc.scalar.activation(diagonal[k % DIAGONALS][:, :], t.ident[:, :], ACT.Identity, scale=weight[b][:, k:k + 1]).then_inc(s["diagonal"], 1)

            passes(act, nothing, one, nothing)

        @block.vector
        def _(dve):
            v = nc.vector
            v.memset(zeros[:, :], 0.0).then_inc(s["zeroed"], 1)
            dve.wait_ge(s["zeroed"], 1)
            dve.wait_ge(s["iota_loaded"], 16)
            dve.sem_inc(s["looked_up"], 1)
            dve.sem_inc(s["dotted"], RING)
            dve.sem_inc(s["emptied"], 1)
            dve.sem_inc(s["tile_done"], 1)

            def look_up(n, b, turn, used):
                dve.wait_ge(scores_loaded[b], (turn + 1) * 16)
                dve.sem_inc(s["held_vector"], 1)
                dve.sem_clear(s["vector"])
                done = Steps(dve, s["vector"])
                for c in range(2):
                    given, left = scores[b][:, c, :], rest[:, c, :]
                    done.step(v.max(best[:, c, 0:8], given))
                    done.step(v.max_index(best_at[:, c, 0:8], best[:, c, 0:8], given))
                    done.step(v.match_replace(left, best[:, c, 0:8], given, LOWEST))
                    done.step(v.max(best[:, c, 8:16], left))
                    done.step(v.max_index(best_at[:, c, 8:16], best[:, c, 8:16], left))
                done.step(v.tensor_tensor(sums[:, :, :], best[:, 0, :].unsqueeze(2).to_broadcast([P, TOPK, TOPK]),
                                          best[:, 1, :].unsqueeze(1).to_broadcast([P, TOPK, TOPK]), ALU.add))
                flat = sums[:, :, :].rearrange("p a b -> p (a b)")
                done.step(v.max(top[b][:, 0:8], flat))
                done.step(v.max_index(top_at[:, 0:8], top[b][:, 0:8], flat))
                done.step(v.match_replace(sums_rest[:, :], top[b][:, 0:8], flat, LOWEST))
                done.step(v.max(top[b][:, 8:16], sums_rest[:, :]))
                done.step(v.max_index(top_at[:, 8:16], top[b][:, 8:16], sums_rest[:, :]))
                done.step(v.tensor_scalar(least[b][:, :], top[b][:, 0:1], -1.0, None, ALU.mult))
                done.step(v.tensor_scalar(place[:, 0, :], top_at[:, :], 4, None, ALU.logical_shift_right))
                done.step(v.tensor_scalar(place[:, 1, :], top_at[:, :], TOPK - 1, None, ALU.bitwise_and))
                for c in range(2):
                    done.step(v.tensor_tensor(chosen[:, :, :], iota[:, :].unsqueeze(1).to_broadcast([P, TOPK, TOPK]),
                                              place[:, c, :].unsqueeze(2).to_broadcast([P, TOPK, TOPK]), ALU.is_equal))
                    done.step(v.tensor_tensor(chosen[:, :, :], chosen[:, :, :],
                                              best_at[:, c, :].unsqueeze(1).to_broadcast([P, TOPK, TOPK]), ALU.mult))
                    done.step(v.tensor_reduce(expert[:, c, :], chosen[:, :, :], AX, ALU.add))
                done.step(v.tensor_scalar(number[:, :], expert[:, 0, :], float(KEYS), t.table_start[:, 0:1], ALU.mult, ALU.add))
                assert done.n == LOOKUP
                if used is not None:
                    dve.wait_ge(s["mixed"], used)
                v.tensor_tensor(index[b][:, :], number[:, :], expert[:, 1, :], ALU.add).then_inc(s["looked_up"], 1)
                dve.wait_ge(s["looked_up"], n + 2)

            look_up(0, 0, 0, None)

            def tile(i):
                dve.wait_ge(s["h_loaded"], (i + 1) * 16)
                dve.sem_inc(s["held_vector"], 1)

            def use(n, b):
                for k in range(TOPK):
                    dve.wait_ge(u_landed[k % RING], (n * TURNS + k // RING + 1) * 16)
                    v.tensor_tensor_reduce(u_rows[k % RING][:, :], u_rows[k % RING][:, :], h[:, :], 1.0, 0.0, ALU.mult, ALU.add,
                                           dots[b][:, k:k + 1]).then_inc(s["dotted"], 1)
                dve.wait_ge(s["powers"], n + 1)
                done = Steps(dve, s["weight_steps"], n * 2)
                done.step(v.reciprocal(inverse[b][:, :], total[b][:, :]))
                dve.wait_ge(s["activated"], n + 1)
                done.step(v.tensor_tensor(active[b][:, :], active[b][:, :], power[b][:, :], ALU.mult))
                v.tensor_scalar(weight[b][:, :], active[b][:, :], inverse[b][:, 0:1], None, ALU.mult).then_inc(s["weighed"], 1)

            def empty(i):
                dve.wait_ge(s["tile_mixed"], i + 1)
                for c in range(2):
                    last = v.tensor_copy(t.peer_sum[:, ds(i, 1), c * 512:(c + 1) * 512], t.bank[c].unsqueeze(1))
                last.then_inc(s["emptied"], 1)

            with dve.Fori(0, TILES) as i:
                tile(i)
                with dve.Fori(0, PAIRS) as j:
                    for b in range(2):
                        n = (i * PAIRS + j) * 2 + b
                        look_up(n + 1, 1 - b, i * PAIRS + j + b, n * TOPK + RING)
                        use(n, b)
                dve.sem_inc(s["tile_done"], 1)
                empty(i)


PEER = ("iota_loaded", "scores_loaded0", "scores_loaded1", "tile_done", "held", "held_pool", "held_vector", "h_loaded", "looked_up", "dotted", "mixed", "zeroed",
        "emptied", "diagonal", "tile_mixed", "powers", "activated", "weighed", "vector", "weight_steps",
        *[f"{n}_landed{k}" for n in "uv" for k in range(8)])


def residual_stage(nc, t, s, before):
    block_stack = ExitStack()
    with block_stack:
        block = block_stack.enter_context(nc.Block())

        @block.gpsimd
        def _(pool):
            clear(pool, before)

        @block.vector
        def _(dve):
            done = Steps(dve, s["steps"])
            done.step(nc.vector.tensor_scalar(t.table_start[:, :], t.table_start[:, :], float(EXPERTS), None, ALU.add))
            for lo, hi in ((0, 1), (1, TILES)):
                x, y = t.x[:, lo:hi, :], t.peer_sum[:, lo:hi, :]
                done.step(nc.vector.tensor_tensor(y, y, t.gate_rows[:, 1, lo:lo + 1, :].to_broadcast([P, hi - lo, D]), ALU.mult))
                done.step(nc.vector.tensor_tensor(x, x, y, ALU.add))


RESIDUAL = ("steps",)


SCRATCH = {"rkv_scratch": (TILES * CORE_ROWS, 3 * W), "rw_scratch": (NTOK, RW_BLOCKS, W), "out_scratch": (2, NTOK, W),
           "h_scratch": (NTOK, D), "score_scratch": (TILES * HEADS + 1, P, 2, KEYS)}
OUTER_STAGES = (("start", ("loaded", "zeroed")), ("finish", ("stored",)))
STAGES = (("modulation", MODULATION), ("norm1", NORM), ("project", PROJECT), ("conv", CONV), ("qk", QK),
          ("attention", ATTENTION), ("rwkv_inputs", RWKV_INPUTS), ("wkv", WKV), ("rwkv_output", RWKV_OUTPUT),
          ("merge", MERGE), ("norm2", NORM), ("peer_query", PEER_QUERY), ("peer", PEER), ("residual", RESIDUAL))
assert len(STAGES) % 2 == 0


def layer_stages(nc, t, stages, layer):
    modulation_stage(nc, t, stages["modulation"], stages["residual"], layer)
    norm_stage(nc, t, stages["norm1"], stages["modulation"], 0)
    with ExitStack() as held:
        def sbuf(stack, name, *shape):
            return stack.enter_context(nc.sbuf_tensor(name, [P, *shape], F32))

        t.y_rw, t.y_conv, t.y_attn = (sbuf(held, n, 4, NTOK) for n in ("y_rw", "y_conv", "y_attn"))
        with ExitStack() as inner:
            t.lora = sbuf(inner, "lora", 3, LORA_W)
            with ExitStack() as inmost:
                t.qkv = sbuf(inmost, "qkv", TILES, 768)
                t.conv_in = sbuf(inmost, "conv_in", 4, CONV_W)
                project_stage(nc, t, stages["project"], stages["norm1"], layer)
                conv_stage(nc, t, stages["conv"], stages["project"], layer)
                t.keys = sbuf(inmost, "keys", 2, 6 * P)
                t.cached_v = sbuf(inmost, "cached_v", P)
                qk_stage(nc, t, stages["qk"], stages["conv"], layer)
                attention_stage(nc, t, stages["attention"], stages["qk"])
            rwkv_inputs_stage(nc, t, stages["rwkv_inputs"], stages["attention"], layer)
        wkv_stage(nc, t, stages["wkv"], stages["rwkv_inputs"], layer)
        rwkv_output_stage(nc, t, stages["rwkv_output"], stages["wkv"], layer)
        merge_stage(nc, t, stages["merge"], stages["rwkv_output"], layer)
    norm_stage(nc, t, stages["norm2"], stages["merge"], 3)
    peer_query_stage(nc, t, stages["peer_query"], stages["norm2"], layer)
    with nc.sbuf_tensor("peer_sum", [P, TILES, D], F32) as t.peer_sum:
        peer_stage(nc, t, stages["peer"], stages["peer_query"], layer)
        residual_stage(nc, t, stages["residual"], stages["peer"])


def build(nc, d):
    with ExitStack() as stack:
        t = Tensors(d)

        def sbuf(name, shape, dtype=F32):
            return stack.enter_context(nc.sbuf_tensor(name, shape, dtype))

        stages = stage_semaphores(nc, stack)
        t.psum = stack.enter_context(nc.psum_tensor("psum", [P, 8, 512], F32))
        t.bank = [t.psum[:, b, :] for b in range(8)]
        t.ident = sbuf("ident_sb", [P, P])
        t.ones = sbuf("ones_sb", [P, P])
        t.cond = sbuf("cond_sb", [P, KD, 2])
        t.mod = sbuf("mod_sb", [P, NMOD * KD, 2])
        t.gate_rows = sbuf("gate_rows_sb", [P, 2, 2, D])
        t.x = sbuf("x_sb", [P, TILES, D])
        t.h = sbuf("h_sb", [P, KD, NTOK])
        t.table_start = sbuf("table_start", [P, 1])
        s = stages["start"]
        with nc.Block() as block:
            @block.sync
            def _(sp):
                sp.dma_start(t.x[:, :, :], d["x"].rearrange("(t p) n -> p t n", p=P)).then_inc(s["loaded"], 16)
                sp.dma_start(t.ident[:, :], d["square_constants"][0, :, :]).then_inc(s["loaded"], 16)
                sp.dma_start(t.ones[:, :], d["square_constants"][1, :, :]).then_inc(s["loaded"], 16)
                sp.dma_start(t.cond[:, :, :], d["cond"]).then_inc(s["loaded"], 16)
                sp.wait_ge(s["loaded"], 64)

            @block.vector
            def _(dve):
                nc.vector.memset(t.table_start[:, :], 0.0).then_inc(s["zeroed"], 1)
                dve.wait_ge(s["zeroed"], 1)
        with nc.Fori(0, DEPTH) as layer:
            layer_stages(nc, t, stages, layer)
        s = stages["finish"]
        with nc.Block() as block:
            @block.sync
            def _(sp):
                sp.dma_start(d["y"].rearrange("(t p) n -> p t n", p=P), t.x[:, :, :]).then_inc(s["stored"], 16)
                sp.wait_ge(s["stored"], 16)


def square_constants():
    i = np.arange(P)
    row, col = i[:, None], i[None, :]
    out = [np.eye(P), np.ones((P, P))]
    for direction in range(2):
        before = (row < col) if direction == 0 else (row > col)
        upto = before | (row == col)
        first = np.broadcast_to((row < P // 2) if direction == 0 else (row >= P // 2), (P, P))
        out += [upto.astype(np.float64) - first, before, upto]
        for level in range(7):
            b = 1 << level
            lo_hi = (row // (2 * b) == col // (2 * b)) & (row // b % 2 == 0) & (col // b % 2 == 1)
            out.append(lo_hi if direction == 0 else lo_hi.T)
    return np.stack([np.asarray(m, np.float32) for m in out])


def rope_rows():
    inverse = (10000.0 ** (-np.arange(0, 32, 2, dtype=np.float32) / 32)).astype(np.float32)
    token = np.arange(LAT)
    out = np.zeros((LAT, 2, HD), np.float32)
    for h, place in enumerate((token // 64, token % 64)):
        angle = place[:, None].astype(np.float32) * inverse
        for c in range(2):
            at = h * 32 + c * 16
            out[:, 0, at:at + 16] = np.cos(angle)
            out[:, 1, at:at + 16] = np.sin(angle) * (1 if c else -1)
    return out.reshape(LAT, 2 * HD)


def kernel(x_prompt, x_sample, c, cache_k, cache_v, state_wkv, c_ctx, w_mod, b_mod, w_in,
           shift_mu_prev, shift_mu_next, rw_w0, rw_w2, rw_a0, rw_a2, rw_g2, rw_k_k, rw_k_a,
           rw_r_k, rw_gn_w, rw_gn_b, w_out_rwkv, conv_w, conv_b, conv_ln_w, conv_ln_b,
           w_out_conv, q_norm, k_norm, w_out_attn, w_o, peer_wq, peer_keys, peer_u, peer_v):
    import concourse.bacc as bacc
    from concourse.bass_utils import run_bass_kernel_spmd

    L = DEPTH
    inputs = {
        "x": np.concatenate([x_prompt[0], x_sample[0]], 0),
        "cond": np.stack([c_ctx, c[0]]).reshape(2, KD, P).transpose(2, 1, 0),
        "w_mod": w_mod,
        "b_mod": b_mod.reshape(L, NMOD * KD, P).transpose(0, 2, 1),
        "w_in": w_in,
        "mu_rows": np.stack([shift_mu_prev, shift_mu_next], 1)[:, :, :3 * W],
        "mu_lora": np.stack([shift_mu_prev, shift_mu_next], 1)[:, :, 3 * W:].reshape(L, 2, 3, P).transpose(0, 3, 1, 2),
        "rw_rows": np.concatenate([rw_w0, rw_a0] + [rows[:, None] for rows in (rw_k_k, rw_k_a, rw_r_k, rw_gn_w, rw_gn_b)], 1),
        "rw_w2": rw_w2.reshape(L, P, W),
        "rw_a2": rw_a2.reshape(L, P, W),
        "rw_g2": rw_g2,
        "conv_taps": conv_w.transpose(0, 2, 1).reshape(L, 4, P, TAPS).transpose(0, 2, 1, 3),
        "conv_rows": np.stack([conv_b, conv_ln_w, conv_ln_b], 1).reshape(L, 3, 4, P).transpose(0, 3, 1, 2),
        "qk_gain": np.concatenate([np.tile(q_norm, (1, HEADS)), np.tile(k_norm, (1, 2))], 1)[:, None],
        "cache_k": cache_k.reshape(L, P, P),
        "cache_v": cache_v.reshape(L, P, P),
        "state_in": state_wkv.reshape(L, 2, HEADS, HD, HD).transpose(0, 1, 2, 4, 3).reshape(L, 2, PAIRS, P, HD),
        "w_out": np.stack([w_out_rwkv, w_out_conv, w_out_attn], 1),
        "w_o": w_o,
        "peer_wq": peer_wq,
        "peer_keys": peer_keys.transpose(0, 2, 4, 1, 3).reshape(L, P, HEADS, KEYS),
        "peer_u": peer_u.reshape(L * EXPERTS, D),
        "peer_v": peer_v.reshape(L * EXPERTS, D),
        "square_constants": square_constants(),
        "halves": np.stack([np.arange(P) < P // 2, np.arange(P) >= P // 2] * 2, 1).astype(np.float32),
        "rope": rope_rows(),
        "iota": np.arange(TOPK, dtype=np.float32),
    }
    inputs = {k: np.ascontiguousarray(v) for k, v in inputs.items()}
    nc = bacc.Bacc("TRN2", target_bir_lowering=False, num_devices=1)
    d = {n: nc.dram_tensor("in_" + n, v.shape, F32, kind="ExternalInput").ap() for n, v in inputs.items()}
    outputs = {"y": (NTOK, D), "new_k": (L, P, P), "new_v": (L, P, P), "state_out": (L, 2, PAIRS, P, HD)}
    for n, shape in outputs.items():
        d[n] = nc.dram_tensor("out_" + n, shape, F32, kind="ExternalOutput").ap()
    for n, shape in SCRATCH.items():
        d[n] = nc.dram_tensor("scratch_" + n, shape, F32, kind="Internal").ap()
    build(nc, d)
    r = run_bass_kernel_spmd(nc, [{"in_" + n: v for n, v in inputs.items()}], core_ids=[0]).results[0]
    state = r["out_state_out"].reshape(L, 2, HEADS, HD, HD).transpose(0, 1, 2, 4, 3)[None]
    return (r["out_y"][None, :CTX], r["out_y"][None, CTX:], r["out_new_k"].reshape(1, L, CTX, 2, HD),
            r["out_new_v"].reshape(1, L, CTX, 2, HD), np.ascontiguousarray(state))
```
